# Optimizing a Trainium2 kernel written in Bass

```python
import jax, jax.numpy as jnp
from jax import lax
import numpy as np

D_MODEL = 1024
BATCH = 1
SEQ = 512
DEPTH = 2
DEC_BATCH = 8
DEC_SEQ = 16
PAST_LEN = 256

CHUNK = 64
MIX_WIDTH = D_MODEL
RET_WIDTH = MIX_WIDTH // 2
CONV_WIDTH = MIX_WIDTH - RET_WIDTH
N_RET_HEADS = 4
RET_HEAD_DIM = RET_WIDTH // N_RET_HEADS
CONV_K = 3
D_FF = 4 * D_MODEL
ROPE_BASE = 10000.0
RMS_EPS = 1e-6
GN_EPS = 1e-5
IN_COLS = 4 * RET_WIDTH + 3 * CONV_WIDTH
SPLITS = [RET_WIDTH, 2 * RET_WIDTH, 3 * RET_WIDTH, 4 * RET_WIDTH,
          4 * RET_WIDTH + CONV_WIDTH, 4 * RET_WIDTH + 2 * CONV_WIDTH]

kernel_name = "hymba_retention_shortconv_stream_step"

def rms_norm(x, w):
    xf = x.astype(jnp.float32)
    y = xf * lax.rsqrt(jnp.mean(xf * xf, axis=-1, keepdims=True) + RMS_EPS)
    return (y * w.astype(jnp.float32)).astype(x.dtype)

def retention_log_decay():
    return jnp.log(1.0 - jnp.exp2(-5.0 - jnp.arange(N_RET_HEADS, dtype=jnp.float32)))

def rope(x, pos):
    half = RET_HEAD_DIM // 2
    inv = ROPE_BASE ** (-jnp.arange(half, dtype=jnp.float32) / half)
    ang = pos.astype(jnp.float32)[:, None] * inv[None, :]
    cos = jnp.cos(ang)[None, :, None, :]
    sin = jnp.sin(ang)[None, :, None, :]
    x1, x2 = x[..., :half], x[..., half:]
    return jnp.concatenate([x1 * cos - x2 * sin, x1 * sin + x2 * cos], axis=-1)

def retention_chunkwise(q, k, v, r0, chunk):
    b, l, h, d = q.shape
    nc = l // chunk

    def to_chunks(t):
        return t.reshape(b, nc, chunk, h, d).transpose(1, 0, 3, 2, 4)

    lg = retention_log_decay()
    idx = jnp.arange(chunk, dtype=jnp.float32)
    diff = idx[:, None] - idx[None, :]
    causal = diff >= 0
    dmat = jnp.where(causal[None], jnp.exp(jnp.where(causal, diff, 0.0)[None] * lg[:, None, None]), 0.0)
    q_dec = jnp.exp((idx[None, :] + 1.0) * lg[:, None])
    k_dec = jnp.exp((chunk - 1.0 - idx[None, :]) * lg[:, None])
    chunk_dec = jnp.exp(chunk * lg)

    def step(r, qkv):
        qc, kc, vc = qkv
        s = jnp.einsum('bhnd,bhmd->bhnm', qc, kc) * dmat[None]
        o = (jnp.einsum('bhnm,bhmv->bhnv', s, vc)
             + jnp.einsum('bhnd,bhdv->bhnv', qc * q_dec[None, :, :, None], r))
        r = (r * chunk_dec[None, :, None, None]
             + jnp.einsum('bhmd,bhmv->bhdv', kc * k_dec[None, :, :, None], vc))
        return r, o

    r_final, o = lax.scan(step, r0, (to_chunks(q), to_chunks(k), to_chunks(v)))
    o = o.transpose(1, 0, 3, 2, 4).reshape(b, l, h, d)
    return o, r_final

def hybrid_layer(x, pos, r0, conv_buf, chunk, ln1_w, w_in, conv_w, ret_norm_w, w_out,
                 ln2_w, w_up, w_down):
    b, l, _ = x.shape
    n = rms_norm(x, ln1_w)
    proj = n @ w_in
    q, k, v, g, gate_b, gate_c, hc = jnp.split(proj, SPLITS, axis=-1)

    shp = (b, l, N_RET_HEADS, RET_HEAD_DIM)
    qf = rope(q.reshape(shp).astype(jnp.float32), pos)
    kf = rope(k.reshape(shp).astype(jnp.float32), pos) * (RET_HEAD_DIM ** -0.5)
    vf = v.reshape(shp).astype(jnp.float32)
    o, r_new = retention_chunkwise(qf, kf, vf, r0.astype(jnp.float32), chunk)
    mu = jnp.mean(o, axis=-1, keepdims=True)
    oc = o - mu
    o = oc * lax.rsqrt(jnp.mean(oc * oc, axis=-1, keepdims=True) + GN_EPS)
    o = o.reshape(b, l, RET_WIDTH) * ret_norm_w.astype(jnp.float32)
    ret_out = (jax.nn.silu(g.astype(jnp.float32)) * o).astype(x.dtype)

    u = gate_c * hc
    padded = jnp.concatenate([conv_buf.astype(u.dtype), u], axis=1)
    z = padded[:, 0:l] * conv_w[:, 0]
    for j in range(1, CONV_K):
        z = z + padded[:, j:j + l] * conv_w[:, j]
    conv_out = gate_b * z
    new_buf = padded[:, l:]

    x = x + jnp.concatenate([ret_out, conv_out], axis=-1) @ w_out

    h2 = rms_norm(x, ln2_w)
    x = x + jnp.square(jax.nn.relu(h2 @ w_up)) @ w_down
    return x, r_new, new_buf

def setup_inputs(seed: int = 0) -> dict:
    key = jax.random.key(seed)
    ks = jax.random.split(key, 13)
    f32 = jnp.float32
    nrm = jax.random.normal
    return {
        "x_prompt": nrm(ks[0], (BATCH, SEQ, D_MODEL), f32),
        "x_sample": nrm(ks[1], (DEC_BATCH, DEC_SEQ, D_MODEL), f32),
        "state_ret": 0.1 * nrm(ks[2], (DEPTH, DEC_BATCH, N_RET_HEADS, RET_HEAD_DIM, RET_HEAD_DIM), f32),
        "state_conv": nrm(ks[3], (DEPTH, DEC_BATCH, CONV_K - 1, CONV_WIDTH), f32),
        "ln1_w": 1.0 + 0.02 * nrm(ks[4], (DEPTH, D_MODEL), f32),
        "w_in": nrm(ks[5], (DEPTH, D_MODEL, IN_COLS), f32) * D_MODEL ** -0.5,
        "conv_w": nrm(ks[6], (DEPTH, CONV_WIDTH, CONV_K), f32) * CONV_K ** -0.5,
        "ret_norm_w": 1.0 + 0.02 * nrm(ks[7], (DEPTH, RET_WIDTH), f32),
        "w_out": nrm(ks[8], (DEPTH, MIX_WIDTH, D_MODEL), f32) * MIX_WIDTH ** -0.5,
        "ln2_w": 1.0 + 0.02 * nrm(ks[9], (DEPTH, D_MODEL), f32),
        "w_mlp_up": nrm(ks[10], (DEPTH, D_MODEL, D_FF), f32) * D_MODEL ** -0.5,
        "w_mlp_down": nrm(ks[11], (DEPTH, D_FF, D_MODEL), f32) * D_FF ** -0.5,
        "ln_f_w": 1.0 + 0.02 * nrm(ks[12], (D_MODEL,), f32),
    }

def reference(x_prompt, x_sample, state_ret, state_conv, ln1_w, w_in, conv_w, ret_norm_w,
              w_out, ln2_w, w_mlp_up, w_mlp_down, ln_f_w):
    b_p, l_p, _ = x_prompt.shape
    b_s, l_s, _ = x_sample.shape
    pos_p = jnp.arange(l_p)
    pos_s = PAST_LEN + jnp.arange(l_s)
    chunk_p = min(CHUNK, l_p)
    chunk_s = l_s

    xp, xs = x_prompt, x_sample
    ret_p, conv_p, ret_s, conv_s = [], [], [], []
    for i in range(DEPTH):
        r0_p = jnp.zeros((b_p, N_RET_HEADS, RET_HEAD_DIM, RET_HEAD_DIM), jnp.float32)
        buf0_p = jnp.zeros((b_p, CONV_K - 1, CONV_WIDTH), x_prompt.dtype)
        xp, rp, bp = hybrid_layer(xp, pos_p, r0_p, buf0_p, chunk_p, ln1_w[i], w_in[i], conv_w[i],
                                  ret_norm_w[i], w_out[i], ln2_w[i], w_mlp_up[i], w_mlp_down[i])
        xs, rs, bs = hybrid_layer(xs, pos_s, state_ret[i], state_conv[i], chunk_s, ln1_w[i], w_in[i],
                                  conv_w[i], ret_norm_w[i], w_out[i], ln2_w[i], w_mlp_up[i],
                                  w_mlp_down[i])
        ret_p.append(rp)
        conv_p.append(bp)
        ret_s.append(rs)
        conv_s.append(bs)

    y_prompt = rms_norm(xp, ln_f_w)
    y_sample = rms_norm(xs, ln_f_w)
    new_ret_prompt = jnp.stack(ret_p).astype(state_ret.dtype)
    new_conv_prompt = jnp.stack(conv_p).astype(state_conv.dtype)
    new_ret_sample = jnp.stack(ret_s).astype(state_ret.dtype)
    new_conv_sample = jnp.stack(conv_s).astype(state_conv.dtype)
    return (y_prompt, y_sample, new_ret_prompt, new_conv_prompt, new_ret_sample, new_conv_sample)


_drawn_inputs = setup_inputs


def setup_inputs(seed=0):
    import zlib

    import numpy as np

    out = dict(_drawn_inputs(seed))
    spreads = {}
    factors = {'ret_norm_w': 5.777, 'ln_f_w': 8.339, 'ln2_w': 3.457}
    for name, (base, spread) in spreads.items():
        noise = np.random.default_rng([zlib.crc32(name.encode()), seed]).standard_normal(out[name].shape)
        drawn = base * np.exp(spread * noise) if base else spread * noise
        out[name] = __import__('jax').numpy.asarray(drawn.astype(out[name].dtype))
    for name, factor in factors.items():
        out[name] = (out[name] * factor).astype(out[name].dtype)
    return out
```

```python
import numpy as np
import concourse.bass as bass
from concourse import mybir
from contextlib import ExitStack

DEPTH, D, TOK, SEQ, NB, NS = 2, 1024, 640, 512, 8, 16
P = 128
NT = TOK // P
SAMPLE = NT - 1
KT = D // P
H, HD, RW, CW = 4, 128, 512, 512
FT = CW // P
HALF = TOK // 2
NBLK = 4 * D // 512
UPAD = SEQ + 2 + NB * (NS + 2)
LN_EPS, GN_EPS = 1e-6, 1e-5

ORDER = [SAMPLE, 0, 1, 2, 3]
W_IN_ORDER = [1, 2, 0, 3, 5, 6, 4]

GROUPS = ([("K", p) for p in range(NT)] + [("V", p) for p in range(NT)] + [("Q", p) for p in range(NT)]
          + [("G", t) for t in range(NT)]
          + [(s, ft, h) for s in "CHB" for ft in range(FT) for h in range(2)]
          + [("O", dh, t) for dh in range(2) for t in range(NT)])
GROUP = {g: n for n, g in enumerate(GROUPS)}
MIX = len(GROUPS)
STAGE_START = [GROUP[x] for x in (("K", 0), ("V", 0), ("Q", 0), ("G", 0), ("C", 0, 0), ("H", 0, 0),
                                  ("B", 0, 0), ("O", 0, 0), ("O", 1, 0))]
MIX_CHUNKS = len(STAGE_START)
UPS, DOWNS = 2 * FT, 2 * NT
PER_BLOCK = UPS + DOWNS
PER_LAYER = MIX + NBLK * PER_BLOCK
CHUNKS = MIX_CHUNKS + 2 * NBLK
UNITS = 2 * CHUNKS
SCALAR_READS = "VC"
MIX_SCALAR = [n for n, g in enumerate(GROUPS) if g[0] in SCALAR_READS]
MIX_VECTOR = [n for n, g in enumerate(GROUPS) if g[0] not in SCALAR_READS]
SCALAR_PER_LAYER = len(MIX_SCALAR) + NBLK * UPS
VECTOR_PER_LAYER = len(MIX_VECTOR) + NBLK * DOWNS

TURNS = ([("n1", p, c) for p in range(NT) for c in range(2)] + [("k", p) for p in range(NT)]
         + [("q", p) for p in range(NT)] + [("o", t) for t in range(NT)] + [("past",), ("tail",)]
         + [("n2", p, c) for p in range(NT) for c in range(2)])
TURN = {x: n for n, x in enumerate(TURNS)}
SPLIT_TURNS = [n for n, x in enumerate(TURNS) if x[0] in ("n1", "n2", "o")]


def split_turns_to(n):
    return sum(m <= n for m in SPLIT_TURNS)


GAPS = {("Q", 2): [("S", 0)],
        ("Q", 3): [("S", 1), ("so", 0), ("sa", 0), ("sb", 0)],
        ("Q", 4): [("R", 1), ("Y", 1), ("S", 2), ("so", 1), ("sa", 1), ("sb", 1)],
        ("G", 0): [("R", 2), ("Y", 2), ("S", 3), ("so", 2), ("sa", 2), ("sb", 2)],
        ("G", 1): [("R", 3), ("Y", 3), ("S", 4), ("so", 3), ("sa", 3), ("sb", 3)],
        ("G", 2): [("R", 4), ("Y", 4)]}
SMALLS = [s for gap in GAPS.values() for s in gap]
SMALL = {s: n for n, s in enumerate(SMALLS)}
TURN_AFTER = {**{("K", p): [("n1", p + 2, 0), ("n1", p + 2, 1)] for p in range(3)},
              **{("V", p): [("k", p)] for p in range(NT)},
              ("Q", 1): [("q", 0)], ("Q", 2): [("q", 1)], ("Q", 3): [("q", 2)], ("Q", 4): [("q", 3)],
              ("G", 0): [("q", 4)], ("G", 3): [("o", 0), ("o", 1)], ("G", 4): [("o", 2), ("o", 3)],
              ("C", 0, 0): [("o", 4), ("past",)], ("H", 3, 1): [],
              ("B", 0, 0): [("tail",)],
              **{("O", 1, t): [("n2", t - 2, 0), ("n2", t - 2, 1)] for t in range(2, NT)}}


def up_group(b, j):
    if isinstance(b, int) and b == 0:
        return MIX + j
    return b * PER_BLOCK + (MIX + UPS - PER_BLOCK + j)


def down_group(d, j):
    if isinstance(d, int) and d == NBLK - 1:
        return PER_LAYER - DOWNS + j
    return d * PER_BLOCK + (MIX + 2 * UPS + j)


def up_chunk(b):
    return MIX_CHUNKS if isinstance(b, int) and b == 0 else b * 2 + (MIX_CHUNKS - 1)


def down_chunk(d):
    return CHUNKS - 1 if isinstance(d, int) and d == NBLK - 1 else d * 2 + (MIX_CHUNKS + 2)


def parity_up(b_is_first):
    return MIX_CHUNKS % 2 if b_is_first else (MIX_CHUNKS + 1) % 2


def parity_down(d_is_last):
    return (CHUNKS - 1) % 2 if d_is_last else (MIX_CHUNKS + 2) % 2


def program(nc, x_p, x_s, state_ret, state_conv, norm_rows, ln2_w, w_in, conv_w, ret_w, w_out, w_up, w_down,
            consts, y_p, y_s, new_ret_p, new_conv_p, new_ret_s, new_conv_s):
    f32, f32r = mybir.dt.float32, mybir.dt.float32r
    ALU, ACT = mybir.AluOpType, mybir.ActivationFunctionType
    gamma = [1.0 - 2.0 ** (-5 - h) for h in range(H)]

    ctx = ExitStack()
    with ctx:
        KB = 1024
        at = [(nc.sbuf_base + 31) // 32 * 32]

        def place(name, shape, dt, offset=None):
            size = 4 * int(np.prod(shape[1:]))
            if offset is None:
                offset = at[0]
                at[0] += (size + 31) // 32 * 32
            return nc.alloc_sbuf_tensor_at(name, shape, dt, offset=offset)

        def region(size):
            offset = at[0]
            at[0] += size
            return offset

        x = place("x", [P, NT, D], f32)
        norm_hi = place("norm_hi", [P, KT, TOK], f32r)
        norm_lo = place("norm_lo", [P, KT, TOK], f32r)
        w_hi = place("w_hi", [P, 2, 2, 4, 512], f32r)
        w_lo = place("w_lo", [P, 2, 2, 4, 512], f32r)
        w_raw = place("w_raw", [P, 2, 4, 512], f32)

        inner_at = region(2 * KT * TOK * 4)
        quarter = FT * TOK * 4
        inner_hi = place("inner_hi", [P, KT, TOK], f32r, inner_at)
        inner_lo = place("inner_lo", [P, KT, TOK], f32r, inner_at + 2 * quarter)
        k_rot = place("k_rot", [P, NT, RW], f32, inner_at)
        kT = place("kT", [P, NT, H, P], f32, inner_at + 2 * quarter)
        past_state = [place(f"past_state{i}", [P, NB, HD], f32, inner_at + quarter + i * 4 * KB) for i in range(2)]
        scores_s = place("scores_s", [P, H, P], f32, inner_at + quarter + 8 * KB)
        q_spread = place("q_spread", [P, NB, P], f32, inner_at + 3 * quarter)
        v_spread = place("v_spread", [P, NB, HD], f32, inner_at + 3 * quarter + 4 * KB)
        scores_p = place("scores_p", [P, H, P], f32, inner_at + 3 * quarter + 8 * KB)

        vo_at = region(FT * UPAD * 4 + 32)
        v = place("v", [P, NT, RW], f32, vo_at)
        o = place("o", [P, NT, RW], f32, vo_at)
        u = place("u", [P, FT, UPAD], f32, vo_at)
        relu = place("relu", [P, 4, HALF], f32, vo_at)

        temp_at = region(10 * KB)
        xn = place("xn", [P, 2, D], f32, temp_at)
        q_rot = place("q_rot", [P, 2, RW], f32, temp_at)
        gate = place("gate", [P, 2, RW], f32, temp_at)
        qT_s = place("qT_s", [P, H, P], f32, temp_at + 4 * KB)
        qT_p = place("qT_p", [P, 2, H, P], f32, temp_at + 6 * KB)
        z = place("z", [P, 2, TOK], f32, temp_at)

        rows_at = region(2 * KB)
        rope_tmp = place("rope_tmp", [P, RW], f32, rows_at)
        conv_rows = place("conv_rows", [P, CW], f32, rows_at)

        norm_row = place("norm_row", [P, D], f32)
        ret_row = place("ret_row", [P, RW], f32)
        ret_state = place("ret_state", [P, H, HD], f32)
        NCONST = consts.shape[1]
        const = place("const", [P, NCONST], f32)
        conv_taps = place("conv_taps", [P, FT, 3], f32)
        sums = place("sums", [P, NT], f32)
        var = place("var", [P, NT], f32)
        rstd = place("rstd", [P, NT], f32)
        group_parts = place("group_parts", [P, H, 6], f32)
        group_mv = place("group_mv", [P, H, 2], f32)
        group_var = place("group_var", [P, H], f32)
        group_rstd = place("group_rstd", [P, H], f32)
        tail = place("tail", [P, FT, 2 + 2 * NB], f32)
        minus_half = place("minus_half", [P, H], f32)
        assert at[0] <= nc.sbuf_usable_end, (at[0], nc.sbuf_usable_end)

        c0 = 0
        identity = const[:, 0:P]
        c0 += P
        cos_sin = const[:, c0:c0 + NT * HD].rearrange("p (t c f) -> p t c f", t=NT, c=2)
        c0 += NT * HD
        mask_p = const[:, c0:c0 + RW]
        mask_s = const[:, c0 + RW:c0 + 2 * RW]
        c0 += 2 * RW
        q_decay = const[:, c0:c0 + 2 * H].rearrange("p (c h) -> p c h", c=2)
        k_decay = const[:, c0 + 2 * H:c0 + 4 * H].rearrange("p (c h) -> p c h", c=2)
        stream_of = const[:, c0 + 4 * H:c0 + 4 * H + NB]

        bank = [ctx.enter_context(nc.psum_tensor(f"bank{i}", [P, 512], f32)) for i in range(8)]
        mix_bank = [bank[i] for i in (0, 1, 2)]
        turn_bank = [bank[i] for i in (3, 4)]
        small_bank = [bank[i] for i in (5, 6, 7)]
        mlp_bank = mix_bank + small_bank

        class Signal:
            def __init__(self, name, per_layer, start=0):
                self.sem, self.per_layer, self.start = ctx.enter_context(nc.semaphore(name)), per_layer, start

            def at(self, layer, n):
                return layer * self.per_layer + (n + self.start)

        consts_in = ctx.enter_context(nc.semaphore("consts_in"))
        x_in = [ctx.enter_context(nc.semaphore(f"x_in{t}")) for t in range(NT)]
        y_out = [ctx.enter_context(nc.semaphore(f"y_out{i}")) for i in range(2)]
        raw_in = [Signal(f"raw_in{s}", 16 * CHUNKS) for s in range(2)]
        norm_row_in = Signal("norm_row_in", 32)
        layer_rows_in = Signal("layer_rows_in", 32)
        past_in = Signal("past_in", 16)
        state_in = [Signal(f"state_in{i}", 32) for i in range(2)]
        state_out = [Signal(f"state_out{i}", 32) for i in range(2)]
        layer_out = Signal("layer_out", 48)

        group_done = Signal("group_done", PER_LAYER, start=1)
        turned = Signal("turned", len(TURNS))
        small_done = Signal("small_done", len(SMALLS))
        w_hi_ready = Signal("w_hi_ready", UNITS)
        w_lo_ready = Signal("w_lo_ready", UNITS, start=2)
        scalar_read = Signal("scalar_read", SCALAR_PER_LAYER)
        vector_read = Signal("vector_read", VECTOR_PER_LAYER, start=1)
        turn_read = Signal("turn_read", len(TURNS))
        turn_lo = Signal("turn_lo", len(SPLIT_TURNS))
        small_read = Signal("small_read", len(SMALLS))
        squares = Signal("squares", 2 * NT)
        rstd_ready = Signal("rstd_ready", 2 * NT)
        xn_ready = Signal("xn_ready", 2 * NT)
        k_rotated = Signal("k_rotated", NT)
        q_rotated = Signal("q_rotated", NT)
        k_decayed = Signal("k_decayed", NT)
        q_spread_ready = Signal("q_spread_ready", H)
        v_spread_ready = Signal("v_spread_ready", H)
        group_stats = Signal("group_stats", NT)
        group_rstd_ready = Signal("group_rstd_ready", NT)
        o_normed = Signal("o_normed", NT)
        o_scaled = Signal("o_scaled", NT)
        sigmoid_ready = Signal("sigmoid_ready", NT)
        o_gated = Signal("o_gated", NT)
        tail_ready = Signal("tail_ready", 1)
        tap0_ready = Signal("tap0_ready", FT)
        mix_hi = Signal("mix_hi", 2 * FT)
        mix_lo = Signal("mix_lo", 2 * FT)
        squared = Signal("squared", NBLK * UPS)
        hidden_hi = Signal("hidden_hi", NBLK * UPS)
        hidden_lo = Signal("hidden_lo", NBLK * UPS)
        rope_step = Signal("rope_step", 2 * NT)
        stats_step = Signal("stats_step", NT)
        tap_step = Signal("tap_step", 2 * FT)
        eps_step = Signal("eps_step", 3 * NT)
        spread_zero = Signal("spread_zero", 1)
        half_ready = ctx.enter_context(nc.semaphore("half_ready"))

        STATS = [1, 2, 3, 0, 4]
        STAT = {p: n for n, p in enumerate(STATS)}

        def sample_cols(t2):
            return t2.rearrange("p (b s) -> p b s", b=NB)

        def u_sample(ft, tap):
            return u[:, ft, SEQ + 2:UPAD].rearrange("p (b s) -> p b s", b=NB)[:, :, tap:tap + NS]

        block = ctx.enter_context(nc.Block())

        def load_x(eng, p):
            t = ORDER[p]
            src = x_s.rearrange("b s d -> (b s) d") if t == SAMPLE else x_p[0, t * P:(t + 1) * P, :]
            eng.dma_start(x[:, t], src).then_inc(x_in[t], 16)

        waits_passed = ctx.enter_context(nc.semaphore("waits_passed"))

        def settle(eng):
            eng.sem_inc(waits_passed, 1)

        @block.sync
        def _(sp):
            for_w_in = w_in.rearrange("l (a k p) (s c) -> l s a p k c", a=2, p=P, c=512)
            for_w_out = w_out.rearrange("l (a k p) (s c) -> l s a p k c", a=2, p=P, c=512)
            for_up = w_up.rearrange("l (a k p) (s c) -> l s a p k c", a=2, p=P, c=512)
            for_down = w_down.rearrange("l (s k p) (a c) -> l s a p k c", k=4, p=P, c=512)

            def load_unit(layer, chunk, half, src, index):
                sp.wait_ge(w_lo_ready.sem, w_lo_ready.at(layer, chunk * 2 + (half - 1)))
                settle(sp)
                sp.dma_start(w_raw[:, half],
                             src[bass.ds(layer, 1), bass.ds(index, 1), half].rearrange("l s p k c -> (l s p) k c")
                             ).then_inc(raw_in[half].sem, 16)

            def load_norm_row(table, index):
                sp.dma_start(norm_row[:], table[bass.ds(index, 1), :].to_broadcast([P, D])).then_inc(
                    norm_row_in.sem, 16)

            def load_state(layer, h):
                sp.dma_start(past_state[h % 2][:],
                             state_ret[bass.ds(layer, 1), :, h].rearrange("l b d v -> (l d) b v")
                             ).then_inc(state_in[h % 2].sem, 16)

            def store_state(layer, h):
                sp.wait_ge(small_read.sem, small_read.at(layer, SMALL["sb", h] + 1))
                sp.dma_start(new_ret_s[bass.ds(layer, 1), :, h].rearrange("l b d v -> (l d) b v"),
                             past_state[h % 2][:]).then_inc(state_out[h % 2].sem, 16)

            load_x(sp, 0)
            sp.dma_start(norm_row[:], norm_rows[0:1, :].to_broadcast([P, D])).then_inc(norm_row_in.sem, 16)
            sp.dma_start(const[:], consts).then_inc(consts_in, 16)
            load_x(sp, 1)
            with sp.Fori(0, DEPTH) as layer:
                def units(chunk, src, index):
                    for half in range(2):
                        load_unit(layer, chunk, half, src, index)

                units(0, for_w_in, W_IN_ORDER[0])
                sp.dma_start(ret_row[:], ret_w[bass.ds(layer, 1), :].to_broadcast([P, RW])).then_inc(
                    layer_rows_in.sem, 16)
                sp.dma_start(conv_taps[:], conv_w[bass.ds(layer, 1)].rearrange("l (f p) j -> (l p) f j", p=P)
                             ).then_inc(layer_rows_in.sem, 16)
                sp.wait_ge(group_done.sem, group_done.at(layer, 0))
                for h in range(2):
                    load_state(layer, h)
                units(1, for_w_in, W_IN_ORDER[1])
                units(2, for_w_in, W_IN_ORDER[2])
                units(3, for_w_in, W_IN_ORDER[3])
                sp.wait_ge(xn_ready.sem, xn_ready.at(layer, NT))
                load_norm_row(ln2_w, layer)
                load_unit(layer, 4, 0, for_w_in, W_IN_ORDER[4])
                load_unit(layer, 4, 1, for_w_in, W_IN_ORDER[4])
                for h in range(2):
                    store_state(layer, h)
                    sp.wait_ge(state_out[h].sem, state_out[h].at(layer, 16))
                    load_state(layer, h + 2)
                    load_unit(layer, 5, h, for_w_in, W_IN_ORDER[5])
                sp.wait_ge(q_rotated.sem, q_rotated.at(layer, NT))
                sp.dma_start(conv_rows[0:2 * NB, :], state_conv[bass.ds(layer, 1)].rearrange("l b r c -> (l b r) c")
                             ).then_inc(past_in.sem, 16)
                store_state(layer, 2)
                store_state(layer, 3)
                units(6, for_w_in, W_IN_ORDER[6])
                sp.wait_ge(small_read.sem, small_read.at(layer, SMALL["R", 4] + 1))
                sp.dma_start(new_ret_p[bass.ds(layer, 1), 0].rearrange("l h d v -> (l d) h v"), ret_state[:]
                             ).then_inc(layer_out.sem, 16)
                units(7, for_w_out, 0)
                units(8, for_w_out, 1)
                sp.wait_ge(turn_read.sem, turn_read.at(layer, TURN["tail",] + 1))
                sp.dma_start(new_conv_p[bass.ds(layer, 1), 0].rearrange("l r c -> (l r) c"), conv_rows[0:2, :]
                             ).then_inc(layer_out.sem, 16)
                sp.dma_start(new_conv_s[bass.ds(layer, 1)].rearrange("l b r c -> (l b r) c"),
                             conv_rows[2:2 + 2 * NB, :]).then_inc(layer_out.sem, 16)
                units(up_chunk(0), for_up, 0)
                with sp.Fori(0, NBLK // 2 - 1) as turn:
                    for b in range(2):
                        units(up_chunk(turn * 2 + (b + 1)), for_up, turn * 2 + (b + 1))
                        units(down_chunk(turn * 2 + b), for_down, turn * 2 + b)
                sp.wait_ge(xn_ready.sem, xn_ready.at(layer, 2 * NT))
                load_norm_row(norm_rows, layer + 1)
                units(up_chunk(NBLK - 1), for_up, NBLK - 1)
                units(down_chunk(NBLK - 2), for_down, NBLK - 2)
                units(down_chunk(NBLK - 1), for_down, NBLK - 1)
                sp.wait_ge(layer_out.sem, layer_out.at(layer, 48))
                settle(sp)
                for i in range(2):
                    sp.wait_ge(state_out[i].sem, state_out[i].at(layer, 32))
                    settle(sp)

            for t in range(NT):
                sp.wait_ge(xn_ready.sem, 2 * NT * DEPTH + t + 1)
                dst = y_s.rearrange("b s d -> (b s) d") if t == SAMPLE else y_p[0, t * P:(t + 1) * P, :]
                sp.dma_start(dst, xn[:, t % 2]).then_inc(y_out[t % 2], 16)
            for i in range(2):
                sp.wait_ge(y_out[i], 16 * ((NT + 1 - i) // 2))

        @block.tensor
        def _(pe):
            three = ((0, 0), (0, 1), (1, 0))
            norms, inners, ws = (norm_hi, norm_lo), (inner_hi, inner_lo), (w_hi, w_lo)

            pe.sem_inc(group_done.sem, 1)
            pe.wait_ge(consts_in, 16)

            def wait_unit(layer, chunk, half):
                pe.wait_ge(w_hi_ready.sem, w_hi_ready.at(layer, chunk * 2 + (half + 1)))
                pe.wait_ge(w_lo_ready.sem, w_lo_ready.at(layer, chunk * 2 + (half + 1)))

            def tokens_product(out, tile, act, k_of, w_of, before=None):
                ks = k_of
                for n, k in enumerate(ks):
                    if before:
                        before(n)
                    for m, (a, b) in enumerate(three):
                        mm = pe.matmul(out, act[a][:, k, tile * P:(tile + 1) * P], w_of(b, n),
                                       start=(n == 0 and m == 0), stop=(n == len(ks) - 1 and m == 2))
                return mm

            def features_product(out, ft, half, par, before=None):
                for k in range(KT):
                    if before:
                        before(k)
                    for m, (a, b) in enumerate(three):
                        mm = pe.matmul(out, ws[a][:, par, k // 4, k % 4, ft * P:(ft + 1) * P],
                                       norms[b][:, k, half * HALF:(half + 1) * HALF],
                                       start=(k == 0 and m == 0), stop=(k == KT - 1 and m == 2))
                return mm

            def turn(layer, what):
                n = TURN[what]
                if n >= 2:
                    pe.wait_ge(turn_read.sem, turn_read.at(layer, n - 1))
                    if n - 2 in SPLIT_TURNS:
                        pe.wait_ge(turn_lo.sem, turn_lo.at(layer, split_turns_to(n - 2)))
                out = turn_bank[n % 2]
                kind = what[0]
                if kind in ("n1", "n2"):
                    p, c = what[1:]
                    if c == 0:
                        pe.wait_ge(xn_ready.sem, xn_ready.at(layer, NT * (kind == "n2") + p + 1))
                    src = [xn[:, p % 2, (4 * c + i) * P:(4 * c + i + 1) * P] for i in range(4)]
                elif kind == "k":
                    pe.wait_ge(k_rotated.sem, k_rotated.at(layer, what[1] + 1))
                    src = [k_rot[:, ORDER[what[1]], i * P:(i + 1) * P] for i in range(4)]
                elif kind == "q":
                    pe.wait_ge(q_rotated.sem, q_rotated.at(layer, what[1] + 1))
                    src = [q_rot[:, what[1] % 2, i * P:(i + 1) * P] for i in range(4)]
                elif kind == "o":
                    pe.wait_ge(o_gated.sem, o_gated.at(layer, what[1] + 1))
                    src = [o[:, what[1], i * P:(i + 1) * P] for i in range(4)]
                if kind == "past":
                    pe.wait_ge(past_in.sem, past_in.at(layer, 16))
                    settle(pe)
                    for i in range(FT):
                        mm = pe.transpose(out[:, i * 2 * NB:(i + 1) * 2 * NB], conv_rows[0:2 * NB, i * P:(i + 1) * P],
                                          identity[0:2 * NB, 0:2 * NB])
                elif kind == "tail":
                    pe.wait_ge(tail_ready.sem, tail_ready.at(layer, 1))
                    for i in range(FT):
                        mm = pe.transpose(out[0:2 + 2 * NB, i * P:(i + 1) * P], tail[:, i], identity)
                else:
                    for i in range(4):
                        mm = pe.transpose(out[:, i * P:(i + 1) * P], src[i], identity)
                mm.then_inc(turned.sem, 1)

            def small(layer, what):
                n = SMALL[what]
                out = small_bank[n % 3]
                kind, p = what
                needs = [n - 2]
                if kind == "Y":
                    needs += [SMALL["S", p] + 1] + ([SMALL["R", p - 1] + 1] if p >= 2 else [])
                if kind == "so":
                    needs += [SMALL["S", 0] + 1]
                if max(needs) >= 1:
                    pe.wait_ge(small_read.sem, small_read.at(layer, max(needs)))
                if kind == "S":
                    pe.wait_ge(turn_read.sem, turn_read.at(layer, TURN["q", p] + 1))
                    for h in range(H):
                        qT = qT_s[:, h] if p == 0 else qT_p[:, p % 2, h]
                        mm = pe.matmul(out[:, h * P:(h + 1) * P], kT[:, ORDER[p], h], qT, start=True, stop=True)
                elif kind == "R":
                    pe.wait_ge(k_decayed.sem, k_decayed.at(layer, p + 1))
                    for h in range(H):
                        mm = pe.matmul(out[:, h * HD:(h + 1) * HD], k_rot[:, ORDER[p], h * HD:(h + 1) * HD],
                                       v[:, ORDER[p], h * HD:(h + 1) * HD], start=True, stop=True)
                elif kind == "Y":
                    for h in range(H):
                        cols = out[:, h * HD:(h + 1) * HD]
                        mm = pe.matmul(cols, scores_p[:, h], v[:, ORDER[p], h * HD:(h + 1) * HD],
                                       start=True, stop=(p == 1))
                        if p >= 2:
                            mm = pe.matmul(cols, qT_p[:, p % 2, h], ret_state[:, h], start=False, stop=True)
                elif kind == "so":
                    h = p
                    pe.wait_ge(q_spread_ready.sem, q_spread_ready.at(layer, h + 1))
                    pe.wait_ge(state_in[h % 2].sem, state_in[h % 2].at(layer, 16 * (h // 2 + 1)))
                    pe.matmul(out[:, 0:HD], scores_s[:, h], v[:, SAMPLE, h * HD:(h + 1) * HD], start=True, stop=False)
                    for b in range(NB):
                        mm = pe.matmul(out[:, 0:HD], q_spread[:, b], past_state[h % 2][:, b],
                                       start=False, stop=(b == NB - 1))
                else:
                    h, c = p, int(kind == "sb")
                    pe.wait_ge(v_spread_ready.sem, v_spread_ready.at(layer, h + 1))
                    if (h, c) == (0, 0):
                        pe.wait_ge(k_decayed.sem, k_decayed.at(layer, 1))
                    mm = pe.matmul(out[:], k_rot[:, SAMPLE, h * HD:(h + 1) * HD], v_spread[:, 4 * c:4 * c + 4],
                                   start=True, stop=True)
                mm.then_inc(small_done.sem, 1)

            with pe.Fori(0, DEPTH) as layer:
                for p in range(2):
                    for c in range(2):
                        turn(layer, ("n1", p, c))
                for n, g in enumerate(GROUPS):
                    stage, chunk = g[0], max(c for c in range(MIX_CHUNKS) if STAGE_START[c] <= n)
                    par, out = chunk % 2, mix_bank[n % 3]
                    if n >= 3:
                        if n - 3 in MIX_SCALAR:
                            pe.wait_ge(scalar_read.sem, scalar_read.at(layer, MIX_SCALAR.index(n - 3) + 1))
                        else:
                            pe.wait_ge(vector_read.sem, vector_read.at(layer, MIX_VECTOR.index(n - 3) + 1))
                    if stage == "K":
                        last = TURN["n1", g[1], 1]
                        pe.wait_ge(turn_read.sem, turn_read.at(layer, last + 1))
                        pe.wait_ge(turn_lo.sem, turn_lo.at(layer, split_turns_to(last)))

                    def weights_there(k, first=(n == STAGE_START[chunk]), chunk=chunk, stage=stage):
                        if first and k % 4 == 0:
                            wait_unit(layer, chunk, k // 4)
                        if first and chunk == 7:
                            if k == 0:
                                pe.wait_ge(turn_read.sem, turn_read.at(layer, TURN["o", NT - 1] + 1))
                                pe.wait_ge(turn_lo.sem, turn_lo.at(layer, split_turns_to(TURN["o", NT - 1])))
                            if k >= FT:
                                pe.wait_ge(mix_hi.sem, mix_hi.at(layer, 2 * (k - FT + 1)))
                                pe.wait_ge(mix_lo.sem, mix_lo.at(layer, 2 * (k - FT + 1)))

                    if stage in "KVQGO":
                        tile = {"O": g[-1], "G": g[1]}.get(stage, ORDER[g[1]] if stage in "KVQ" else None)
                        act = inners if stage == "O" else norms
                        mm = tokens_product(out[:], tile, act, range(KT),
                                            lambda b, k: ws[b][:, par, k // 4, k % 4], weights_there)
                    else:
                        mm = features_product(out[:, 0:HALF], g[1], g[2], par, weights_there)
                    mm.then_inc(group_done.sem, 1)
                    for s in GAPS.get(g, []):
                        small(layer, s)
                    for s in TURN_AFTER.get(g, []):
                        turn(layer, s)

                def up_block(b):
                    first = isinstance(b, int) and b == 0
                    par, start = parity_up(first), 0 if first else UPS
                    for j in range(UPS):
                        half, ft = divmod(j, FT)
                        if first and j < 3:
                            pe.wait_ge(vector_read.sem, vector_read.at(layer, len(MIX_VECTOR) - 2 + j))
                        if not first and j < 6:
                            pe.wait_ge(vector_read.sem, vector_read.at(
                                layer, b * DOWNS + (len(MIX_VECTOR) - DOWNS - 5 + j)))
                        if not (first and j < 6):
                            pe.wait_ge(scalar_read.sem, scalar_read.at(layer, b * UPS + (len(MIX_SCALAR) - 5 + j)))
                        if first and ft == 0:
                            last = TURN["n2", 2 if half == 0 else NT - 1, 1]
                            pe.wait_ge(turn_read.sem, turn_read.at(layer, last + 1))
                            pe.wait_ge(turn_lo.sem, turn_lo.at(layer, split_turns_to(last)))

                        def weights_there(k, j=j):
                            if j == 0 and k % 4 == 0:
                                wait_unit(layer, up_chunk(b), k // 4)

                        mm = features_product(mlp_bank[(start + j) % 6][:, 0:HALF], ft, half, par, weights_there)
                        mm.then_inc(group_done.sem, 1)
                        if first and j < 2:
                            turn(layer, ("n2", 3 + j, 0))
                            turn(layer, ("n2", 3 + j, 1))

                def down_block(d, buf):
                    last = isinstance(d, int) and d == NBLK - 1
                    par, start = parity_down(last), (2 * UPS + (NBLK - 1) * PER_BLOCK - UPS + DOWNS - DOWNS
                                                     if last else 2 * UPS)
                    start = (PER_LAYER - MIX - DOWNS) if last else 2 * UPS
                    for j in range(DOWNS):
                        dh, t = divmod(j, NT)
                        if j < 6 and not last:
                            pe.wait_ge(scalar_read.sem, scalar_read.at(
                                layer, d * UPS + (len(MIX_SCALAR) + UPS + 3 + j)))
                        else:
                            pe.wait_ge(vector_read.sem, vector_read.at(
                                layer, d * DOWNS + (len(MIX_VECTOR) - 5 + j)))
                        if j == 0:
                            pe.wait_ge(hidden_hi.sem, hidden_hi.at(layer, d * UPS + UPS))
                            pe.wait_ge(hidden_lo.sem, hidden_lo.at(layer, d * UPS + UPS))
                        if t == 0:
                            wait_unit(layer, down_chunk(d), dh)
                        mm = tokens_product(mlp_bank[(start + j) % 6][:], t, inners,
                                            range(buf * FT, buf * FT + FT),
                                            lambda b, k: ws[b][:, par, dh, k])
                        mm.then_inc(group_done.sem, 1)

                up_block(0)
                with pe.Fori(0, NBLK // 2 - 1) as turn_i:
                    for b in range(2):
                        up_block(turn_i * 2 + (b + 1))
                        down_block(turn_i * 2 + b, b)
                up_block(NBLK - 1)
                down_block(NBLK - 2, 0)
                down_block(NBLK - 1, 1)

        @block.scalar
        def _(act):
            def split_unit(layer, chunk, half, par, groups_before):
                act.wait_ge(raw_in[half].sem, raw_in[half].at(layer, (chunk + 1) * 16))
                act.wait_ge(group_done.sem, group_done.at(layer, groups_before))
                nc.scalar.activation(w_hi[:, par, half], w_raw[:, half], ACT.Copy).then_inc(w_hi_ready.sem, 1)

            def split_chunk(layer, chunk, par, groups_before):
                for half in range(2):
                    split_unit(layer, chunk, half, par, groups_before)

            def square(layer, base, p, tile):
                if p >= 2:
                    turns = TURN["n1" if base == 0 else "n2", p - 2, 1]
                    act.wait_ge(turned.sem, turned.at(layer, turns + 1))
                nc.scalar.activation(xn[:, p % 2], x[:, tile], ACT.Square,
                                     accum_out=sums[:, p:p + 1]).then_inc(squares.sem, 1)

            def read_turn(layer, what):
                n = TURN[what]
                src, kind = turn_bank[n % 2], what[0]
                act.wait_ge(turned.sem, turned.at(layer, n + 1))
                if kind in ("n1", "n2"):
                    p, c = what[1:]
                    tile = ORDER[p] if kind == "n1" else p
                    dst = norm_hi[:, 4 * c:4 * c + 4, tile * P:(tile + 1) * P]
                    src = src[:].rearrange("p (k t) -> p k t", k=4)
                elif kind == "k":
                    dst, src = kT[:, ORDER[what[1]]].rearrange("p h t -> p (h t)"), src[:]
                elif kind == "q":
                    q = qT_s[:] if what[1] == 0 else qT_p[:, what[1] % 2]
                    dst, src = q.rearrange("p h t -> p (h t)"), src[:]
                elif kind == "o":
                    dst = inner_hi[:, 0:FT, what[1] * P:(what[1] + 1) * P]
                    src = src[:].rearrange("p (k t) -> p k t", k=4)
                elif kind == "past":
                    for ft in range(FT):
                        to = u[:, ft, SEQ + 2:UPAD].rearrange("p (b s) -> p b s", b=NB)[:, :, 0:2]
                        of = src[:, ft * 2 * NB:(ft + 1) * 2 * NB].rearrange("p (b r) -> p b r", b=NB)
                        ins = nc.scalar.activation(to, of, ACT.Copy)
                    ins.then_inc(turn_read.sem, 1)
                    return
                else:
                    dst, src = conv_rows[0:2 + 2 * NB, :], src[0:2 + 2 * NB, :]
                nc.scalar.activation(dst, src, ACT.Copy).then_inc(turn_read.sem, 1)

            for p in range(2, NT):
                load_x(act, p)
            with act.Fori(0, DEPTH) as layer:
                def square1(p):
                    act.wait_ge(x_in[ORDER[p]], 16)
                    act.wait_ge(vector_read.sem, vector_read.at(layer, 0))
                    square(layer, 0, p, ORDER[p])

                square1(0)
                square1(1)
                split_unit(layer, 0, 0, 0, 0)
                for c in range(2):
                    read_turn(layer, ("n1", 0, c))
                split_unit(layer, 0, 1, 0, 0)
                for p in range(2, NT):
                    square1(p)
                    for c in range(2):
                        read_turn(layer, ("n1", p - 1, c))
                    if p == 3:
                        split_chunk(layer, 1, 1, 0)
                for c in range(2):
                    read_turn(layer, ("n1", NT - 1, c))

                split_chunk(layer, 2, 0, STAGE_START[1])
                for p in range(NT):
                    n = GROUP["V", p]
                    act.wait_ge(group_done.sem, group_done.at(layer, n + 1))
                    nc.scalar.activation(v[:, ORDER[p]], mix_bank[n % 3][:], ACT.Copy).then_inc(scalar_read.sem, 1)
                    read_turn(layer, ("k", p))

                split_chunk(layer, 3, 1, STAGE_START[2])
                for p in range(4):
                    if p == 3:
                        act.wait_ge(small_done.sem, small_done.at(layer, SMALL["Y", 1] + 1))
                    read_turn(layer, ("q", p))

                split_chunk(layer, 4, 0, STAGE_START[3])
                for t in range(NT):
                    n = GROUP["G", t]
                    act.wait_ge(group_done.sem, group_done.at(layer, n + 1))
                    if t >= 2:
                        act.wait_ge(o_gated.sem, o_gated.at(layer, t - 1))
                    nc.scalar.activation(gate[:, (t + 1) % 2], mix_bank[n % 3][:], ACT.Sigmoid
                                         ).then_inc(sigmoid_ready.sem, 1)
                    if t == 0:
                        act.wait_ge(small_done.sem, small_done.at(layer, SMALL["Y", 2] + 1))
                        read_turn(layer, ("q", 4))
                    if t == 3:
                        act.wait_ge(small_read.sem, small_read.at(layer, len(SMALLS)))
                        for s in range(2):
                            read_turn(layer, ("o", s))
                for s in range(2, 4):
                    read_turn(layer, ("o", s))

                split_chunk(layer, 5, 1, STAGE_START[4])
                read_turn(layer, ("o", 4))
                read_turn(layer, ("past",))
                for ft in range(FT):
                    for half in range(2):
                        n = GROUP["C", ft, half]
                        act.wait_ge(group_done.sem, group_done.at(layer, n + 1))
                        src = mix_bank[n % 3]
                        if half == 0:
                            ins = nc.scalar.activation(u[:, ft, 2:2 + HALF], src[:, 0:HALF], ACT.Copy)
                        else:
                            rest = SEQ - HALF
                            nc.scalar.activation(u[:, ft, 2 + HALF:2 + SEQ], src[:, 0:rest], ACT.Copy)
                            ins = nc.scalar.activation(u_sample(ft, 2), sample_cols(src[:, rest:HALF]), ACT.Copy)
                        ins.then_inc(scalar_read.sem, 1)

                split_chunk(layer, 6, 0, STAGE_START[5])

                def first_tap(ft):
                    if ft < 2:
                        act.wait_ge(vector_read.sem, vector_read.at(
                            layer, MIX_VECTOR.index(GROUP["H", ft, 1]) + 1))
                        if ft == 0:
                            act.wait_ge(layer_rows_in.sem, layer_rows_in.at(layer, 32))
                    else:
                        act.wait_ge(vector_read.sem, vector_read.at(
                            layer, MIX_VECTOR.index(GROUP["H", ft, 1]) + 1))
                        act.wait_ge(mix_lo.sem, mix_lo.at(layer, 2 * (ft - 1)))
                    nc.scalar.activation(z[:, ft % 2, 0:SEQ], u[:, ft, 0:SEQ], ACT.Copy,
                                         scale=conv_taps[:, ft, 0:1])
                    nc.scalar.activation(sample_cols(z[:, ft % 2, SEQ:TOK]), u_sample(ft, 0), ACT.Copy,
                                         scale=conv_taps[:, ft, 0:1]).then_inc(tap0_ready.sem, 1)

                first_tap(0)
                first_tap(1)
                split_chunk(layer, 7, 1, STAGE_START[6])
                read_turn(layer, ("tail",))
                for ft in range(FT):
                    for half in range(2):
                        act.wait_ge(vector_read.sem, vector_read.at(
                            layer, MIX_VECTOR.index(GROUP["B", ft, half]) + 1))
                        cols = slice(half * HALF, (half + 1) * HALF)
                        nc.scalar.activation(inner_hi[:, FT + ft, cols], z[:, ft % 2, cols], ACT.Copy
                                             ).then_inc(mix_hi.sem, 1)
                    if ft + 2 < FT:
                        first_tap(ft + 2)

                split_chunk(layer, 8, 0, STAGE_START[7])
                split_chunk(layer, 9, 1, STAGE_START[8])
                for t in range(NT):
                    act.wait_ge(vector_read.sem, vector_read.at(
                        layer, MIX_VECTOR.index(GROUP["O", 1, t]) + 1))
                    square(layer, NT, t, t)
                    if t >= 1:
                        for c in range(2):
                            read_turn(layer, ("n2", t - 1, c))

                def up_block(b, buf, chunk, par, before):
                    split_chunk(layer, chunk, par, before)

                    def hi_part(j):
                        half, ft = divmod(j, FT)
                        act.wait_ge(squared.sem, squared.at(layer, b * UPS + (j + 1)))
                        nc.scalar.activation(inner_hi[:, buf * FT + ft, half * HALF:(half + 1) * HALF],
                                             relu[:, j % 4], ACT.Copy).then_inc(hidden_hi.sem, 1)

                    first = isinstance(b, int) and b == 0
                    for j in range(UPS):
                        act.wait_ge(group_done.sem, group_done.at(layer, up_group(b, j + 1)))
                        if not (first and j < 4):
                            act.wait_ge(hidden_lo.sem, hidden_lo.at(layer, b * UPS + (j - 3)))
                        slot = (0 if first else UPS) + j
                        nc.scalar.activation(relu[:, j % 4], mlp_bank[slot % 6][:, 0:HALF], ACT.Relu
                                             ).then_inc(scalar_read.sem, 1)
                        if j >= 1:
                            hi_part(j - 1)
                    hi_part(UPS - 1)

                for c in range(2):
                    read_turn(layer, ("n2", NT - 1, c))
                up_block(0, 0, 10, 0, up_group(0, 0))
                with act.Fori(0, NBLK // 2 - 1) as i:
                    for b in range(2):
                        up, down = i * 2 + (b + 1), i * 2 + b
                        up_block(up, (b + 1) % 2, down_chunk(down), 1, up_group(up, 0))
                        split_chunk(layer, up_chunk(i * 2 + (b + 2)), 0, down_group(down, 0))
                up_block(NBLK - 1, 1, down_chunk(NBLK - 2), 1, up_group(NBLK - 1, 0))
                split_chunk(layer, down_chunk(NBLK - 1), 0, down_group(NBLK - 2, 0))

            for t in range(NT):
                act.wait_ge(vector_read.sem, vector_read.at(DEPTH, 0))
                if t >= 2:
                    act.wait_ge(y_out[t % 2], 16 * (t // 2))
                nc.scalar.activation(xn[:, t % 2], x[:, t], ACT.Square,
                                     accum_out=sums[:, t:t + 1]).then_inc(squares.sem, 1)

        @block.gpsimd
        def _(pool):
            nc.gpsimd.memset(minus_half[:], -0.5).then_inc(half_ready, 1)
            pool.wait_ge(half_ready, 1)
            pool.wait_ge(consts_in, 16)

            eps_n = [0]

            def rstd_of(layer, count, out, tmp, src, scale, eps, done):
                settle(pool)
                nc.gpsimd.tensor_scalar(tmp, src, scale, eps, ALU.mult, ALU.add).then_inc(eps_step.sem, 1)
                eps_n[0] += 1
                pool.wait_ge(eps_step.sem, eps_step.at(layer, eps_n[0]))
                nc.gpsimd.tensor_tensor(out, tmp, minus_half[:, 0:tmp.shape[1]], ALU.pow).then_inc(done.sem, 1)

            def row_rstd(layer, base, p):
                pool.wait_ge(squares.sem, squares.at(layer, base + p + 1))
                rstd_of(layer, None, rstd[:, p:p + 1], var[:, p:p + 1], sums[:, p:p + 1], 1.0 / D, LN_EPS, rstd_ready)

            def rotate(layer, stage, p, dst, done):
                pool.wait_ge(vector_read.sem, vector_read.at(layer, MIX_VECTOR.index(GROUP[stage, p]) + 1))
                a = dst.rearrange("p (h c f) -> p h c f", h=H, c=2)
                b = rope_tmp[:].rearrange("p (h c f) -> p h c f", h=H, c=2)
                nc.gpsimd.tensor_tensor(a[:, :, 0], a[:, :, 0], b[:, :, 1], ALU.subtract)
                nc.gpsimd.tensor_tensor(a[:, :, 1], a[:, :, 1], b[:, :, 0], ALU.add).then_inc(done.sem, 1)

            def decay_k(layer, p):
                pool.wait_ge(turned.sem, turned.at(layer, TURN["k", p] + 1))
                kk = k_rot[:, ORDER[p]].rearrange("p (h f) -> p h f", h=H)
                nc.gpsimd.tensor_tensor(kk, kk, k_decay[:, int(p == 0)].unsqueeze(2).to_broadcast([P, H, HD]),
                                        ALU.mult).then_inc(k_decayed.sem, 1)

            def spread_q(layer, h):
                pool.wait_ge(turn_read.sem, turn_read.at(layer, TURN["q", 0] + 1))
                if h == 0:
                    pool.wait_ge(spread_zero.sem, spread_zero.at(layer, 1))
                else:
                    pool.wait_ge(small_done.sem, small_done.at(layer, SMALL["so", h - 1] + 1))
                settle(pool)
                ins = nc.gpsimd.tensor_copy(diagonal_blocks(q_spread), sample_cols(qT_s[:, h]))
                ins.then_inc(q_spread_ready.sem, 1)

            def spread_v(layer, h):
                if h >= 1:
                    pool.wait_ge(small_done.sem, small_done.at(layer, SMALL["sb", h - 1] + 1))
                vv = v[:, SAMPLE, h * HD:(h + 1) * HD]
                nc.gpsimd.tensor_tensor(v_spread[:], vv.unsqueeze(1).to_broadcast([P, NB, HD]),
                                        stream_of.unsqueeze(2).to_broadcast([P, NB, HD]), ALU.mult
                                        ).then_inc(v_spread_ready.sem, 1)

            def diagonal_blocks(t):
                a = t[:].rearrange("p b t -> p (b t)")
                a = a[:, 0:NB * (P + NS)] if NB * (P + NS) <= NB * P else a
                return bass.AP(tensor=a.tensor, offset=a.offset, ap=[list(a.ap[0]), [P + NS, NB], [1, NS]])

            def finish_o(layer, p):
                pool.wait_ge(o_normed.sem, o_normed.at(layer, STAT[p] + 1))
                if STAT[p] == 0:
                    pool.wait_ge(layer_rows_in.sem, layer_rows_in.at(layer, 32))
                oo = o[:, ORDER[p]]
                nc.gpsimd.tensor_tensor(oo, oo, ret_row[:], ALU.mult).then_inc(o_scaled.sem, 1)

            def group_norm(layer, p):
                pool.wait_ge(group_stats.sem, group_stats.at(layer, STAT[p] + 1))
                rstd_of(layer, None, group_rstd[:], group_var[:], group_mv[:, :, 1], 1.0, GN_EPS, group_rstd_ready)

            with pool.Fori(0, DEPTH) as layer:
                eps_n[0] = 0
                row_rstd(layer, 0, 0)
                row_rstd(layer, 0, 1)
                pool.wait_ge(group_done.sem, group_done.at(layer, 0))
                settle(pool)
                nc.gpsimd.memset(q_spread[:], 0.0).then_inc(spread_zero.sem, 1)
                for p in range(NT):
                    if p + 2 < NT:
                        row_rstd(layer, 0, p + 2)
                    rotate(layer, "K", p, k_rot[:, ORDER[p]], k_rotated)
                for p in range(NT):
                    decay_k(layer, p)
                pool.wait_ge(scalar_read.sem, scalar_read.at(layer, 1))
                spread_v(layer, 0)
                for p in range(NT):
                    rotate(layer, "Q", p, q_rot[:, p % 2], q_rotated)
                    if p == 1:
                        spread_q(layer, 0)
                spread_q(layer, 1)
                spread_v(layer, 1)
                group_norm(layer, 1)
                finish_o(layer, 1)
                spread_q(layer, 2)
                spread_v(layer, 2)
                group_norm(layer, 2)
                finish_o(layer, 2)
                spread_q(layer, 3)
                spread_v(layer, 3)
                group_norm(layer, 3)
                finish_o(layer, 3)
                group_norm(layer, 0)
                finish_o(layer, 0)
                group_norm(layer, 4)
                finish_o(layer, 4)
                for t in range(NT):
                    row_rstd(layer, NT, t)
                assert eps_n[0] == eps_step.per_layer
            eps_n[0] = 0
            for t in range(NT):
                row_rstd(DEPTH, 0, t)

        @block.vector
        def _(dve):
            dve.sem_inc(w_lo_ready.sem, 2)
            dve.sem_inc(vector_read.sem, 1)
            dve.wait_ge(consts_in, 16)
            f = lambda t: t.bitcast(f32)

            def split_unit(layer, chunk, half, par):
                dve.wait_ge(w_hi_ready.sem, w_hi_ready.at(layer, chunk * 2 + (half + 1)))
                nc.vector.tensor_tensor(w_lo[:, par, half], w_raw[:, half], f(w_hi[:, par, half]), ALU.subtract
                                        ).then_inc(w_lo_ready.sem, 1)

            def split_chunk(layer, chunk, par):
                for half in range(2):
                    split_unit(layer, chunk, half, par)

            def normalise(layer, base, p, tile, row_count):
                dve.wait_ge(rstd_ready.sem, rstd_ready.at(layer, base + p + 1))
                dve.wait_ge(norm_row_in.sem, norm_row_in.at(layer, row_count))
                nc.vector.scalar_tensor_tensor(out=xn[:, p % 2], in0=x[:, tile], scalar=rstd[:, p:p + 1],
                                               in1=norm_row[:], op0=ALU.mult, op1=ALU.mult).then_inc(xn_ready.sem, 1)

            def read_turn_lo(layer, what):
                n = TURN[what]
                src = turn_bank[n % 2][:].rearrange("p (k t) -> p k t", k=4)
                if what[0] == "o":
                    ks, tile, hi, lo = slice(0, FT), what[1], inner_hi, inner_lo
                else:
                    p, c = what[1:]
                    ks, tile = slice(4 * c, 4 * c + 4), ORDER[p] if what[0] == "n1" else p
                    hi, lo = norm_hi, norm_lo
                cols = slice(tile * P, (tile + 1) * P)
                dve.wait_ge(turn_read.sem, turn_read.at(layer, n + 1))
                nc.vector.tensor_tensor(lo[:, ks, cols], src, f(hi[:, ks, cols]), ALU.subtract
                                        ).then_inc(turn_lo.sem, 1)

            def wait_group(layer, n):
                dve.wait_ge(group_done.sem, group_done.at(layer, n + 1))

            def rope(layer, stage, p, dst, done):
                n = GROUP[stage, p]
                src = mix_bank[n % 3][:].rearrange("p (h f) -> p h f", f=HD // 2)
                wait_group(layer, n)
                if stage == "Q" and p >= 2:
                    dve.wait_ge(turned.sem, turned.at(layer, TURN["q", p - 2] + 1))
                tab = [cos_sin[:, ORDER[p], c].unsqueeze(1).to_broadcast([P, 2 * H, HD // 2]) for c in range(2)]
                nc.vector.tensor_tensor(dst.rearrange("p (h f) -> p h f", f=HD // 2), src, tab[0], ALU.mult)
                if (stage, p) != ("K", 0):
                    prev = done.at(layer, p) if p else k_rotated.at(layer, NT)
                    dve.wait_ge((done if p else k_rotated).sem, prev)
                nc.vector.tensor_tensor(rope_tmp[:].rearrange("p (h f) -> p h f", f=HD // 2), src, tab[1], ALU.mult
                                        ).then_inc(vector_read.sem, 1)

            def stats(layer, p):
                tile = ORDER[p]
                last = SMALL["so", H - 1] if p == 0 else SMALL["Y", p]
                dve.wait_ge(small_read.sem, small_read.at(layer, last + 1))
                if STAT[p] >= 1:
                    dve.wait_ge(o_normed.sem, o_normed.at(layer, STAT[p]))
                for h in range(H):
                    ins = nc.vector.bn_stats(group_parts[:, h], o[:, tile, h * HD:(h + 1) * HD])
                ins.then_inc(stats_step.sem, 1)
                dve.wait_ge(stats_step.sem, stats_step.at(layer, STAT[p] + 1))
                settle(dve)
                for h in range(H):
                    ins = nc.vector.bn_aggr(group_mv[:, h], group_parts[:, h])
                ins.then_inc(group_stats.sem, 1)

            def norm_heads(layer, p):
                dve.wait_ge(group_rstd_ready.sem, group_rstd_ready.at(layer, STAT[p] + 1))
                for h in range(H):
                    oo = o[:, ORDER[p], h * HD:(h + 1) * HD]
                    ins = nc.vector.tensor_scalar(oo, oo, group_mv[:, h, 0:1], group_rstd[:, h:h + 1],
                                                  ALU.subtract, ALU.mult)
                ins.then_inc(o_normed.sem, 1)

            def read_small(layer, what):
                n = SMALL[what]
                kind, p = what
                src = small_bank[n % 3]
                dve.wait_ge(small_done.sem, small_done.at(layer, n + 1))
                if kind == "S":
                    dst, mask = (scores_s, mask_s) if p == 0 else (scores_p, mask_p)
                    ins = nc.vector.tensor_tensor(dst[:].rearrange("p h t -> p (h t)"), src[:], mask, ALU.mult)
                elif kind == "R":
                    dve.wait_ge(small_done.sem, small_done.at(layer, SMALL["Y", p] + 1))
                    if p == 1:
                        ins = nc.vector.tensor_copy(ret_state[:].rearrange("p h f -> p (h f)"), src[:])
                    else:
                        dve.wait_ge(small_read.sem, small_read.at(layer, SMALL["R", p - 1] + 1))
                        for h in range(H):
                            ins = nc.vector.scalar_tensor_tensor(
                                out=ret_state[:, h], in0=ret_state[:, h], scalar=gamma[h] ** P,
                                in1=src[:, h * HD:(h + 1) * HD], op0=ALU.mult, op1=ALU.add)
                elif kind == "Y":
                    ins = nc.vector.tensor_tensor(
                        o[:, ORDER[p]].rearrange("p (h f) -> p h f", h=H), src[:].rearrange("p (h f) -> p h f", h=H),
                        q_decay[:, 0].unsqueeze(2).to_broadcast([P, H, HD]), ALU.mult)
                elif kind == "so":
                    dve.wait_ge(v_spread_ready.sem, v_spread_ready.at(layer, p + 1))
                    ins = nc.vector.tensor_scalar(o[:, SAMPLE, p * HD:(p + 1) * HD], src[:, 0:HD],
                                                  q_decay[:, 1, p:p + 1], None, ALU.mult)
                else:
                    h, c = p, int(kind == "sb")
                    if c == 0:
                        dve.wait_ge(state_in[h % 2].sem, state_in[h % 2].at(layer, 16 * (h // 2 + 1)))
                    st = past_state[h % 2][:, 4 * c:4 * c + 4].rearrange("p b f -> p (b f)")
                    ins = nc.vector.scalar_tensor_tensor(out=st, in0=st, scalar=gamma[h] ** NS, in1=src[:],
                                                         op0=ALU.mult, op1=ALU.add)
                ins.then_inc(small_read.sem, 1)

            def gate_o(layer, t):
                n = GROUP["G", t]
                dve.wait_ge(sigmoid_ready.sem, sigmoid_ready.at(layer, t + 1))
                gg = gate[:, (t + 1) % 2]
                nc.vector.tensor_tensor(gg, gg, mix_bank[n % 3][:], ALU.mult).then_inc(vector_read.sem, 1)

            def finish_gate(layer, t):
                dve.wait_ge(vector_read.sem, vector_read.at(layer, MIX_VECTOR.index(GROUP["G", t]) + 1))
                dve.wait_ge(o_scaled.sem, o_scaled.at(layer, STAT[ORDER.index(t)] + 1))
                nc.vector.tensor_tensor(o[:, t], o[:, t], gate[:, (t + 1) % 2], ALU.mult).then_inc(o_gated.sem, 1)

            with dve.Fori(0, DEPTH) as layer:
                normalise(layer, 0, 0, ORDER[0], 16)
                normalise(layer, 0, 1, ORDER[1], 16)
                split_unit(layer, 0, 0, 0)
                for c in range(2):
                    read_turn_lo(layer, ("n1", 0, c))
                split_unit(layer, 0, 1, 0)
                for p in range(NT):
                    if p + 2 < NT:
                        normalise(layer, 0, p + 2, ORDER[p + 2], 16)
                    if p + 1 < NT:
                        for c in range(2):
                            read_turn_lo(layer, ("n1", p + 1, c))
                    rope(layer, "K", p, k_rot[:, ORDER[p]], k_rotated)
                    if p in (2, 3):
                        split_unit(layer, 1, p - 2, 1)

                split_chunk(layer, 2, 0)

                for p in range(NT):
                    rope(layer, "Q", p, q_rot[:, p % 2], q_rotated)
                    if p < 2:
                        split_unit(layer, 3, p, 1)
                    for s in GAPS.get(("Q", p), []):
                        read_small(layer, s)
                stats(layer, 1)
                split_chunk(layer, 4, 0)
                norm_heads(layer, 1)
                gate_o(layer, 0)
                for s in GAPS["G", 0]:
                    read_small(layer, s)
                    if s[0] == "Y":
                        stats(layer, s[1])
                norm_heads(layer, 2)
                finish_gate(layer, 0)
                gate_o(layer, 1)
                for s in GAPS["G", 1]:
                    read_small(layer, s)
                    if s[0] == "Y":
                        stats(layer, s[1])
                norm_heads(layer, 3)
                finish_gate(layer, 1)
                stats(layer, 0)
                gate_o(layer, 2)
                norm_heads(layer, 0)
                for s in GAPS["G", 2]:
                    read_small(layer, s)
                stats(layer, 4)
                finish_gate(layer, 2)
                norm_heads(layer, 4)
                gate_o(layer, 3)
                finish_gate(layer, 3)
                for t in range(2):
                    read_turn_lo(layer, ("o", t))
                gate_o(layer, 4)
                finish_gate(layer, 4)
                for t in range(2, 4):
                    read_turn_lo(layer, ("o", t))

                split_chunk(layer, 5, 1)
                read_turn_lo(layer, ("o", 4))
                nc.vector.memset(u[:, :, 0:2], 0.0)

                for ft in range(FT):
                    for half in range(2):
                        n = GROUP["H", ft, half]
                        wait_group(layer, n)
                        dve.wait_ge(scalar_read.sem, scalar_read.at(
                            layer, MIX_SCALAR.index(GROUP["C", ft, half]) + 1))
                        src = mix_bank[n % 3]
                        if half == 0:
                            uu = u[:, ft, 2:2 + HALF]
                            ins = nc.vector.tensor_tensor(uu, uu, src[:, 0:HALF], ALU.mult)
                        else:
                            rest = SEQ - HALF
                            uu = u[:, ft, 2 + HALF:2 + SEQ]
                            nc.vector.tensor_tensor(uu, uu, src[:, 0:rest], ALU.mult)
                            uu = u_sample(ft, 2)
                            ins = nc.vector.tensor_tensor(uu, uu, sample_cols(src[:, rest:HALF]), ALU.mult)
                        ins.then_inc(vector_read.sem, 1)
                    if ft in (0, 1):
                        split_unit(layer, 6, ft, 0)
                dve.wait_ge(vector_read.sem, vector_read.at(layer, MIX_VECTOR.index(GROUP["H", FT - 1, 1]) + 1))
                nc.vector.tensor_copy(tail[:, :, 0:2], u[:, :, SEQ:SEQ + 2])
                streams = u[:, :, SEQ + 2:UPAD].rearrange("p f (b s) -> p f b s", b=NB)[:, :, :, NS:NS + 2]
                nc.vector.tensor_copy(tail[:, :, 2:].rearrange("p f (b r) -> p f b r", b=NB), streams
                                      ).then_inc(tail_ready.sem, 1)

                def lo_part(ft, half):
                    dve.wait_ge(mix_hi.sem, mix_hi.at(layer, 2 * ft + half + 1))
                    cols = slice(half * HALF, (half + 1) * HALF)
                    nc.vector.tensor_tensor(inner_lo[:, FT + ft, cols], z[:, ft % 2, cols],
                                            f(inner_hi[:, FT + ft, cols]), ALU.subtract).then_inc(mix_lo.sem, 1)

                for ft in range(FT):
                    dve.wait_ge(tap0_ready.sem, tap0_ready.at(layer, ft + 1))
                    zp, zs = z[:, ft % 2, 0:SEQ], sample_cols(z[:, ft % 2, SEQ:TOK])
                    for tap in (1, 2):
                        w = conv_taps[:, ft, tap:tap + 1]
                        nc.vector.scalar_tensor_tensor(out=zp, in0=u[:, ft, tap:tap + SEQ], scalar=w, in1=zp,
                                                       op0=ALU.mult, op1=ALU.add)
                        nc.vector.scalar_tensor_tensor(out=zs, in0=u_sample(ft, tap), scalar=w, in1=zs,
                                                       op0=ALU.mult, op1=ALU.add).then_inc(tap_step.sem, 1)
                        dve.wait_ge(tap_step.sem, tap_step.at(layer, 2 * ft + tap))
                    for half in range(2):
                        n = GROUP["B", ft, half]
                        wait_group(layer, n)
                        zz = z[:, ft % 2, half * HALF:(half + 1) * HALF]
                        nc.vector.tensor_tensor(zz, zz, mix_bank[n % 3][:, 0:HALF], ALU.mult
                                                ).then_inc(vector_read.sem, 1)
                    if ft in (0, 1):
                        split_unit(layer, 7, ft, 1)
                    for half in range(2):
                        lo_part(ft, half)

                def add_into_x(n, src, t, dh):
                    dve.wait_ge(group_done.sem, n)
                    xx = x[:, t, dh * 512:(dh + 1) * 512]
                    nc.vector.tensor_tensor(xx, xx, src[:], ALU.add).then_inc(vector_read.sem, 1)

                for t in range(NT):
                    n = GROUP["O", 0, t]
                    add_into_x(group_done.at(layer, n + 1), mix_bank[n % 3], t, 0)
                    if t in (0, 1):
                        split_unit(layer, 8, t, 0)
                for t in range(NT):
                    n = GROUP["O", 1, t]
                    add_into_x(group_done.at(layer, n + 1), mix_bank[n % 3], t, 1)
                    if t >= 1:
                        normalise(layer, NT, t - 1, t - 1, 32)
                    if t >= 2:
                        for c in range(2):
                            read_turn_lo(layer, ("n2", t - 2, c))
                    if t in (0, 1):
                        split_unit(layer, 9, t, 1)
                normalise(layer, NT, NT - 1, NT - 1, 32)
                for t in range(NT - 2, NT):
                    for c in range(2):
                        read_turn_lo(layer, ("n2", t, c))

                def up_block(b, buf, chunk, par):
                    def lo_part(j):
                        half, ft = divmod(j, FT)
                        cols = slice(half * HALF, (half + 1) * HALF)
                        dve.wait_ge(hidden_hi.sem, hidden_hi.at(layer, b * UPS + (j + 1)))
                        nc.vector.tensor_tensor(inner_lo[:, buf * FT + ft, cols], relu[:, j % 4],
                                                f(inner_hi[:, buf * FT + ft, cols]), ALU.subtract
                                                ).then_inc(hidden_lo.sem, 1)

                    for j in range(UPS):
                        dve.wait_ge(scalar_read.sem, scalar_read.at(
                            layer, b * UPS + (len(MIX_SCALAR) + j + 1)))
                        nc.vector.tensor_tensor(relu[:, j % 4], relu[:, j % 4], relu[:, j % 4], ALU.mult
                                                ).then_inc(squared.sem, 1)
                        if j >= 1:
                            lo_part(j - 1)
                        if j in (0, 1):
                            split_unit(layer, chunk, j, par)
                    lo_part(UPS - 1)

                def down_block(d, split=None):
                    last = isinstance(d, int) and d == NBLK - 1
                    start = (PER_LAYER - MIX - DOWNS) if last else 2 * UPS
                    for j in range(DOWNS):
                        dh, t = divmod(j, NT)
                        add_into_x(group_done.at(layer, down_group(d, j + 1)), mlp_bank[(start + j) % 6], t, dh)
                        if split is not None and j in (0, 1):
                            split_unit(layer, split, j, 0)

                up_block(0, 0, 10, 0)
                with dve.Fori(0, NBLK // 2 - 1) as i:
                    for b in range(2):
                        up_block(i * 2 + (b + 1), (b + 1) % 2, down_chunk(i * 2 + b), 1)
                        down_block(i * 2 + b, up_chunk(i * 2 + (b + 2)))
                up_block(NBLK - 1, 1, down_chunk(NBLK - 2), 1)
                down_block(NBLK - 2, down_chunk(NBLK - 1))
                down_block(NBLK - 1)

            for t in range(NT):
                dve.wait_ge(rstd_ready.sem, rstd_ready.at(DEPTH, t + 1))
                dve.wait_ge(norm_row_in.sem, norm_row_in.at(DEPTH, 16))
                nc.vector.scalar_tensor_tensor(out=xn[:, t % 2], in0=x[:, t], scalar=rstd[:, t:t + 1],
                                               in1=norm_row[:], op0=ALU.mult, op1=ALU.mult).then_inc(xn_ready.sem, 1)


def shape_constants():
    pos = np.concatenate([np.arange(SEQ), np.tile(256 + np.arange(NS), NB)]).astype(np.float32)
    half = HD // 2
    inv = (10000.0 ** (-np.arange(half, dtype=np.float64) / half)).astype(np.float32)
    ang = (pos[:, None] * inv[None, :]).astype(np.float64)
    cos_sin = np.stack([np.cos(ang), np.sin(ang)], 1).reshape(NT, P, HD).transpose(1, 0, 2)
    g = 1.0 - 2.0 ** (-5.0 - np.arange(H))
    m = np.arange(P)
    scale = HD ** -0.5
    masks, q_decay, k_decay = [], [], []
    for chunk in (P, NS):
        i = m % chunk
        same = (m[:, None] // chunk == m[None, :] // chunk) & (m[:, None] <= m[None, :])
        masks.append((scale * g[None, :, None] ** -(i[:, None, None] + 1.0) * same[:, None, :]).reshape(P, H * P))
        q_decay.append(g[None, :] ** (i[:, None] + 1.0))
        k_decay.append(scale * g[None, :] ** (chunk - 1.0 - i[:, None]))
    stream = (m[:, None] // NS == np.arange(NB)[None, :])
    return np.concatenate([np.eye(P), cos_sin.reshape(P, NT * HD), *masks, *q_decay, *k_decay, stream],
                          1).astype(np.float32)


def kernel(**inputs):
    import concourse.bacc as bacc
    from concourse.bass_utils import run_bass_kernel_spmd

    a = {k: np.ascontiguousarray(v) for k, v in inputs.items()}
    a["norm_rows"] = np.concatenate([a.pop("ln1_w"), a.pop("ln_f_w")[None, :]], 0)
    a["consts"] = shape_constants()
    nc = bacc.Bacc("TRN2", target_bir_lowering=False, num_devices=1, dynamic_dma_scratch_size=1024)
    names = ["x_prompt", "x_sample", "state_ret", "state_conv", "norm_rows", "ln2_w", "w_in", "conv_w",
             "ret_norm_w", "w_out", "w_mlp_up", "w_mlp_down", "consts"]
    args = [nc.dram_tensor("in_" + n, a[n].shape, mybir.dt.float32, kind="ExternalInput").ap() for n in names]
    outs = [("y_p", (1, SEQ, D)), ("y_s", (NB, NS, D)), ("ret_p", (DEPTH, 1, H, HD, HD)), ("conv_p", (DEPTH, 1, 2, CW)),
            ("ret_s", (DEPTH, NB, H, HD, HD)), ("conv_s", (DEPTH, NB, 2, CW))]
    args += [nc.dram_tensor("out_" + n, s, mybir.dt.float32, kind="ExternalOutput").ap() for n, s in outs]
    program(nc, *args)
    r = run_bass_kernel_spmd(nc, [{"in_" + n: a[n] for n in names}], core_ids=[0])
    return tuple(r.results[0]["out_" + n] for n, _ in outs)
```

```python
import numpy as np
import concourse.bass as bass
from concourse import mybir
from contextlib import ExitStack

DEPTH, D, TOK, SEQ, NB, NS = 2, 1024, 640, 512, 8, 16
P = 128
NT = TOK // P
SAMPLE = NT - 1
KT = D // P
H, HD, RW, CW = 4, 128, 512, 512
FT = CW // P
HALF = TOK // 2
NBLK = 4 * D // 512
UPAD = SEQ + 2 + NB * (NS + 2)
LN_EPS, GN_EPS = 1e-6, 1e-5

ORDER = [SAMPLE, 0, 1, 2, 3]
W_IN_ORDER = [1, 2, 0, 3, 5, 6, 4]

GROUPS = ([("K", p) for p in range(NT)] + [("V", p) for p in range(NT)] + [("Q", p) for p in range(NT)]
          + [("G", t) for t in range(NT)]
          + [(s, ft, h) for s in "CHB" for ft in range(FT) for h in range(2)]
          + [("O", dh, t) for dh in range(2) for t in range(NT)])
GROUP = {g: n for n, g in enumerate(GROUPS)}
MIX = len(GROUPS)
STAGE_START = [GROUP[x] for x in (("K", 0), ("V", 0), ("Q", 0), ("G", 0), ("C", 0, 0), ("H", 0, 0),
                                  ("B", 0, 0), ("O", 0, 0), ("O", 1, 0))]
MIX_CHUNKS = len(STAGE_START)
UPS, DOWNS = 2 * FT, 2 * NT
PER_BLOCK = UPS + DOWNS
PER_LAYER = MIX + NBLK * PER_BLOCK
CHUNKS = MIX_CHUNKS + 2 * NBLK
WARMING = 7
PIECES = 4
SCALAR_READS = "VC"
MIX_SCALAR = [n for n, g in enumerate(GROUPS) if g[0] in SCALAR_READS]
MIX_VECTOR = [n for n, g in enumerate(GROUPS) if g[0] not in SCALAR_READS]
SCALAR_PER_LAYER = len(MIX_SCALAR) + NBLK * UPS
VECTOR_PER_LAYER = len(MIX_VECTOR) + NBLK * DOWNS


def made(chunk, half, piece=PIECES - 1):
    if isinstance(chunk, int) and chunk == 0:
        return half * PIECES + piece + 1
    return chunk * 2 + (half + 1 + 2 * (PIECES - 1))


PARTS = 2 * CHUNKS + 2 * (PIECES - 1)

TURNS = ([("n1", p, c) for p in range(NT) for c in range(2)] + [("k", p) for p in range(NT)]
         + [("q", p) for p in range(NT)] + [("o", t) for t in range(NT)] + [("past",), ("tail",)]
         + [("n2", p, c) for p in range(NT) for c in range(2)])
TURN = {x: n for n, x in enumerate(TURNS)}
SPLIT_TURNS = [n for n, x in enumerate(TURNS) if x[0] in ("n1", "n2", "o")]


def split_turns_to(n):
    return sum(m <= n for m in SPLIT_TURNS)


GAPS = {("Q", 2): [("S", 0)],
        ("Q", 3): [("S", 1), ("so", 0), ("sa", 0), ("sb", 0)],
        ("Q", 4): [("Y", 1), ("R", 1), ("so", 1), ("S", 2), ("sa", 1), ("sb", 1)],
        ("G", 0): [("Y", 2), ("R", 2), ("so", 2), ("S", 3), ("sa", 2), ("sb", 2)],
        ("G", 1): [("Y", 3), ("R", 3), ("so", 3), ("S", 4), ("sa", 3), ("sb", 3)],
        ("G", 2): [("Y", 4), ("R", 4)]}
SMALLS = [s for gap in GAPS.values() for s in gap]
SMALL = {s: n for n, s in enumerate(SMALLS)}
TURN_AFTER = {**{("V", p): [("k", p)] for p in range(NT)},
              ("Q", 1): [("q", 0)], ("Q", 2): [("q", 1)], ("Q", 3): [("q", 2)], ("Q", 4): [("q", 3)],
              ("G", 0): [("q", 4)], ("G", 3): [("o", 0), ("o", 1)], ("G", 4): [("o", 2), ("o", 3)],
              ("C", 0, 0): [("o", 4), ("past",)],
              ("B", 0, 0): [("tail",)],
              **{("O", 1, t): [("n2", t - 1, 0), ("n2", t - 1, 1)] for t in range(1, NT)}}


def up_group(b, j):
    if isinstance(b, int) and b == 0:
        return MIX + j
    return b * PER_BLOCK + (MIX + UPS - PER_BLOCK + j)


def down_group(d, j):
    if isinstance(d, int) and d == NBLK - 1:
        return PER_LAYER - DOWNS + j
    return d * PER_BLOCK + (MIX + 2 * UPS + j)


def up_chunk(b):
    return MIX_CHUNKS if isinstance(b, int) and b == 0 else b * 2 + (MIX_CHUNKS - 1)


def down_chunk(d):
    return CHUNKS - 1 if isinstance(d, int) and d == NBLK - 1 else d * 2 + (MIX_CHUNKS + 2)


def parity_up(b_is_first):
    return MIX_CHUNKS % 2 if b_is_first else (MIX_CHUNKS + 1) % 2


def parity_down(d_is_last):
    return (CHUNKS - 1) % 2 if d_is_last else (MIX_CHUNKS + 2) % 2


def program(nc, x_p, x_s, state_ret, state_conv, norm_rows, ln2_w, w_in, conv_w, ret_w, w_out, w_up, w_down,
            consts, y_p, y_s, new_ret_p, new_conv_p, new_ret_s, new_conv_s):
    f32, f32r = mybir.dt.float32, mybir.dt.float32r
    ALU, ACT = mybir.AluOpType, mybir.ActivationFunctionType
    gamma = [1.0 - 2.0 ** (-5 - h) for h in range(H)]

    ctx = ExitStack()
    with ctx:
        KB = 1024
        at = [(nc.sbuf_base + 31) // 32 * 32]

        def place(name, shape, dt, offset=None):
            size = 4 * int(np.prod(shape[1:]))
            if offset is None:
                offset = at[0]
                at[0] += (size + 31) // 32 * 32
            return nc.alloc_sbuf_tensor_at(name, shape, dt, offset=offset)

        def region(size):
            offset = at[0]
            at[0] += size
            return offset

        x = place("x", [P, NT, D], f32)
        norm_hi = place("norm_hi", [P, KT, TOK], f32r)
        norm_lo = place("norm_lo", [P, KT, TOK], f32r)
        w_hi = place("w_hi", [P, 2, 2, 4, 512], f32r)
        w_lo = place("w_lo", [P, 2, 2, 4, 512], f32r)
        w_raw = place("w_raw", [P, 2, 4, 512], f32)

        inner_at = region(2 * KT * TOK * 4)
        quarter = FT * TOK * 4
        inner_hi = place("inner_hi", [P, KT, TOK], f32r, inner_at)
        inner_lo = place("inner_lo", [P, KT, TOK], f32r, inner_at + 2 * quarter)
        k_rot = place("k_rot", [P, NT, RW], f32, inner_at)
        kT = place("kT", [P, NT, H, P], f32, inner_at + 2 * quarter)
        past_state = [place(f"past_state{i}", [P, NB, HD], f32, inner_at + quarter + i * 4 * KB) for i in range(2)]
        scores_s = place("scores_s", [P, H, P], f32, inner_at + quarter + 8 * KB)
        q_spread = place("q_spread", [P, NB, P], f32, inner_at + 3 * quarter)
        v_spread = place("v_spread", [P, NB, HD], f32, inner_at + 3 * quarter + 4 * KB)
        scores_p = place("scores_p", [P, H, P], f32, inner_at + 3 * quarter + 8 * KB)

        squares_out = place("squares_out", [P, 2, D], f32, inner_at)

        vo_at = region(FT * UPAD * 4 + 32)
        v = place("v", [P, NT, RW], f32, vo_at)
        o = place("o", [P, NT, RW], f32, vo_at)
        u = place("u", [P, FT, UPAD], f32, vo_at)
        relu = place("relu", [P, 4, HALF], f32, vo_at)

        temp_at = region(10 * KB)
        xn = place("xn", [P, 2, D], f32, temp_at)
        q_rot = place("q_rot", [P, 2, RW], f32, temp_at)
        gate = place("gate", [P, 2, RW], f32, temp_at)
        qT_s = place("qT_s", [P, H, P], f32, temp_at + 4 * KB)
        qT_p = place("qT_p", [P, 2, H, P], f32, temp_at + 6 * KB)
        z = place("z", [P, 2, TOK], f32, temp_at)

        rows_at = region(2 * KB)
        rope_tmp = place("rope_tmp", [P, RW], f32, rows_at)
        conv_rows = place("conv_rows", [P, CW], f32, rows_at)

        norm_row = place("norm_row", [P, D], f32)
        ret_row = place("ret_row", [P, RW], f32)
        ret_state = place("ret_state", [P, H, HD], f32)
        NCONST = consts.shape[1]
        const = place("const", [P, NCONST], f32)
        conv_taps = place("conv_taps", [P, FT, 3], f32)
        sums = place("sums", [P, NT], f32)
        var = place("var", [P, NT], f32)
        rstd = place("rstd", [P, NT], f32)
        group_parts = place("group_parts", [P, H, 6], f32)
        group_mv = place("group_mv", [P, H, 2], f32)
        group_var = place("group_var", [P, H], f32)
        group_rstd = place("group_rstd", [P, H], f32)
        tail = place("tail", [P, FT, 2 + 2 * NB], f32)
        minus_half = place("minus_half", [P, H], f32)
        assert at[0] <= nc.sbuf_usable_end, (at[0], nc.sbuf_usable_end)

        c0 = 0
        identity = const[:, 0:P]
        c0 += P
        cos_sin = const[:, c0:c0 + NT * HD].rearrange("p (t c f) -> p t c f", t=NT, c=2)
        c0 += NT * HD
        mask_p = const[:, c0:c0 + RW]
        mask_s = const[:, c0 + RW:c0 + 2 * RW]
        c0 += 2 * RW
        q_decay = const[:, c0:c0 + 2 * H].rearrange("p (c h) -> p c h", c=2)
        k_decay = const[:, c0 + 2 * H:c0 + 4 * H].rearrange("p (c h) -> p c h", c=2)
        stream_of = const[:, c0 + 4 * H:c0 + 4 * H + NB]

        bank = [ctx.enter_context(nc.psum_tensor(f"bank{i}", [P, 512], f32)) for i in range(8)]
        mix_bank = [bank[i] for i in (0, 1, 2)]
        turn_bank = [bank[i] for i in (3, 4)]
        small_bank = [bank[i] for i in (5, 6, 7)]
        mlp_bank = mix_bank + small_bank

        class Signal:
            def __init__(self, name, per_layer, start=0):
                self.sem, self.per_layer, self.start = ctx.enter_context(nc.semaphore(name)), per_layer, start

            def at(self, layer, n):
                assert not isinstance(n, int) or n + self.start > 0
                return layer * self.per_layer + (n + self.start)

        identity_in = ctx.enter_context(nc.semaphore("identity_in"))
        consts_in = ctx.enter_context(nc.semaphore("consts_in"))
        x_in = [ctx.enter_context(nc.semaphore(f"x_in{t}")) for t in range(NT)]
        y_out = ctx.enter_context(nc.semaphore("y_out"))
        raw_in = [Signal(f"raw_in{s}", 16 * CHUNKS) for s in range(2)]
        norm_row_in = Signal("norm_row_in", 32)
        layer_rows_in = Signal("layer_rows_in", 32)
        past_in = Signal("past_in", 16)
        state_in = [Signal(f"state_in{i}", 32) for i in range(2)]
        state_out = [Signal(f"state_out{i}", 32) for i in range(2)]
        layer_out = Signal("layer_out", 48)

        group_done = Signal("group_done", PER_LAYER, start=1)
        turned = Signal("turned", len(TURNS))
        small_done = Signal("small_done", len(SMALLS))
        w_hi_ready = Signal("w_hi_ready", PARTS)
        w_lo_ready = Signal("w_lo_ready", PARTS)
        scalar_read = Signal("scalar_read", SCALAR_PER_LAYER)
        vector_read = Signal("vector_read", VECTOR_PER_LAYER, start=1)
        turn_read = Signal("turn_read", len(TURNS))
        turn_lo = Signal("turn_lo", len(SPLIT_TURNS))
        small_read = Signal("small_read", len(SMALLS))
        squares = Signal("squares", 2 * NT)
        rstd_ready = Signal("rstd_ready", 2 * NT)
        xn_ready = Signal("xn_ready", 2 * NT)
        k_rotated = Signal("k_rotated", NT)
        q_rotated = Signal("q_rotated", NT)
        k_decayed = Signal("k_decayed", NT)
        q_spread_ready = Signal("q_spread_ready", H)
        v_spread_ready = Signal("v_spread_ready", H)
        group_stats = Signal("group_stats", NT)
        group_rstd_ready = Signal("group_rstd_ready", NT)
        o_normed = Signal("o_normed", NT)
        o_scaled = Signal("o_scaled", NT)
        sigmoid_ready = Signal("sigmoid_ready", NT)
        o_gated = Signal("o_gated", NT)
        tail_ready = Signal("tail_ready", 1)
        tap0_ready = Signal("tap0_ready", FT)
        mix_hi = Signal("mix_hi", 2 * FT)
        mix_lo = Signal("mix_lo", 2 * FT)
        squared = Signal("squared", NBLK * UPS)
        hidden_hi = Signal("hidden_hi", NBLK * UPS)
        hidden_lo = Signal("hidden_lo", NBLK * UPS)
        stats_step = Signal("stats_step", NT)
        tap_step = Signal("tap_step", 2 * FT)
        eps_step = Signal("eps_step", 3 * NT, start=2)
        spread_zero = Signal("spread_zero", 1)
        half_ready = ctx.enter_context(nc.semaphore("half_ready"))

        STATS = [1, 2, 3, 0, 4]
        STAT = {p: n for n, p in enumerate(STATS)}

        def sample_cols(t2):
            return t2.rearrange("p (b s) -> p b s", b=NB)

        def u_sample(ft, tap):
            return u[:, ft, SEQ + 2:UPAD].rearrange("p (b s) -> p b s", b=NB)[:, :, tap:tap + NS]

        block = ctx.enter_context(nc.Block())

        def load_x(eng, p):
            t = ORDER[p]
            src = x_s.rearrange("b s d -> (b s) d") if t == SAMPLE else x_p[0, t * P:(t + 1) * P, :]
            eng.dma_start(x[:, t], src).then_inc(x_in[t], 16)

        waits_passed = ctx.enter_context(nc.semaphore("waits_passed"))

        def settle(eng):
            eng.sem_inc(waits_passed, 1)

        @block.sync
        def _(sp):
            for_w_in = w_in.rearrange("l (a k p) (s c) -> l s a p k c", a=2, p=P, c=512)
            for_w_out = w_out.rearrange("l (a k p) (s c) -> l s a p k c", a=2, p=P, c=512)
            for_up = w_up.rearrange("l (a k p) (s c) -> l s a p k c", a=2, p=P, c=512)
            for_down = w_down.rearrange("l (s k p) (a c) -> l s a p k c", k=4, p=P, c=512)

            def load_unit(layer, chunk, half, src, index):
                if chunk is not None:
                    sp.wait_ge(w_lo_ready.sem, w_lo_ready.at(layer, made(chunk - 1, half)))
                    settle(sp)
                sp.dma_start(w_raw[:, half],
                             src[bass.ds(layer, 1), bass.ds(index, 1), half].rearrange("l s p k c -> (l s p) k c")
                             ).then_inc(raw_in[half].sem, 16)

            def load_norm_row(table, index):
                sp.dma_start(norm_row[:], table[bass.ds(index, 1), :].to_broadcast([P, D])).then_inc(
                    norm_row_in.sem, 16)

            def load_state(layer, h):
                sp.dma_start(past_state[h % 2][:],
                             state_ret[bass.ds(layer, 1), :, h].rearrange("l b d v -> (l d) b v")
                             ).then_inc(state_in[h % 2].sem, 16)

            def store_state(layer, h):
                sp.wait_ge(small_read.sem, small_read.at(layer, SMALL["sb", h] + 1))
                sp.dma_start(new_ret_s[bass.ds(layer, 1), :, h].rearrange("l b d v -> (l d) b v"),
                             past_state[h % 2][:]).then_inc(state_out[h % 2].sem, 16)

            load_x(sp, 0)
            sp.dma_start(norm_row[:], norm_rows[0:1, :].to_broadcast([P, D])).then_inc(norm_row_in.sem, 16)
            load_unit(0, None, 0, for_w_in, W_IN_ORDER[0])
            load_x(sp, 1)
            load_unit(0, None, 1, for_w_in, W_IN_ORDER[0])
            load_x(sp, 2)
            sp.dma_start(const[:, P:], consts[:, P:]).then_inc(consts_in, 16)
            load_x(sp, 3)
            load_x(sp, 4)
            with sp.Fori(0, DEPTH) as layer:
                def units(chunk, src, index):
                    for half in range(2):
                        load_unit(layer, chunk, half, src, index)

                sp.dma_start(ret_row[:], ret_w[bass.ds(layer, 1), :].to_broadcast([P, RW])).then_inc(
                    layer_rows_in.sem, 16)
                sp.dma_start(conv_taps[:], conv_w[bass.ds(layer, 1)].rearrange("l (f p) j -> (l p) f j", p=P)
                             ).then_inc(layer_rows_in.sem, 16)
                sp.wait_ge(group_done.sem, group_done.at(layer, 0))
                for h in range(2):
                    load_state(layer, h)
                units(1, for_w_in, W_IN_ORDER[1])
                units(2, for_w_in, W_IN_ORDER[2])
                units(3, for_w_in, W_IN_ORDER[3])
                sp.wait_ge(xn_ready.sem, xn_ready.at(layer, NT))
                load_norm_row(ln2_w, layer)
                load_unit(layer, 4, 0, for_w_in, W_IN_ORDER[4])
                load_unit(layer, 4, 1, for_w_in, W_IN_ORDER[4])
                for h in range(2):
                    store_state(layer, h)
                    sp.wait_ge(state_out[h].sem, state_out[h].at(layer, 16))
                    load_state(layer, h + 2)
                    load_unit(layer, 5, h, for_w_in, W_IN_ORDER[5])
                sp.wait_ge(q_rotated.sem, q_rotated.at(layer, NT))
                sp.dma_start(conv_rows[0:2 * NB, :], state_conv[bass.ds(layer, 1)].rearrange("l b r c -> (l b r) c")
                             ).then_inc(past_in.sem, 16)
                store_state(layer, 2)
                store_state(layer, 3)
                units(6, for_w_in, W_IN_ORDER[6])
                sp.wait_ge(small_read.sem, small_read.at(layer, SMALL["R", 4] + 1))
                sp.dma_start(new_ret_p[bass.ds(layer, 1), 0].rearrange("l h d v -> (l d) h v"), ret_state[:]
                             ).then_inc(layer_out.sem, 16)
                units(7, for_w_out, 0)
                units(8, for_w_out, 1)
                sp.wait_ge(turn_read.sem, turn_read.at(layer, TURN["tail",] + 1))
                sp.dma_start(new_conv_p[bass.ds(layer, 1), 0].rearrange("l r c -> (l r) c"), conv_rows[0:2, :]
                             ).then_inc(layer_out.sem, 16)
                sp.dma_start(new_conv_s[bass.ds(layer, 1)].rearrange("l b r c -> (l b r) c"),
                             conv_rows[2:2 + 2 * NB, :]).then_inc(layer_out.sem, 16)
                units(up_chunk(0), for_up, 0)
                with sp.Fori(0, NBLK // 2 - 1) as turn:
                    for b in range(2):
                        units(up_chunk(turn * 2 + (b + 1)), for_up, turn * 2 + (b + 1))
                        units(down_chunk(turn * 2 + b), for_down, turn * 2 + b)
                sp.wait_ge(xn_ready.sem, xn_ready.at(layer, 2 * NT))
                load_norm_row(norm_rows, layer + 1)
                units(up_chunk(NBLK - 1), for_up, NBLK - 1)
                units(down_chunk(NBLK - 2), for_down, NBLK - 2)
                units(down_chunk(NBLK - 1), for_down, NBLK - 1)
                with sp.If(layer < DEPTH - 1):
                    next_layer = nc.s_assert_within(
                        layer + 1, 0, DEPTH - 1,
                        skip_runtime_bounds_check_because="the branch is taken for layer < DEPTH - 1 only")
                    for half in range(2):
                        sp.wait_ge(w_lo_ready.sem, w_lo_ready.at(layer, made(CHUNKS - 1, half)))
                        settle(sp)
                        load_unit(next_layer, None, half, for_w_in, W_IN_ORDER[0])
                sp.wait_ge(layer_out.sem, layer_out.at(layer, 48))
                settle(sp)
                for i in range(2):
                    sp.wait_ge(state_out[i].sem, state_out[i].at(layer, 32))
                    settle(sp)

            for p in range(NT):
                t = ORDER[p]
                sp.wait_ge(xn_ready.sem, xn_ready.at(DEPTH, p + 1))
                dst = y_s.rearrange("b s d -> (b s) d") if t == SAMPLE else y_p[0, t * P:(t + 1) * P, :]
                if p < NT - 1:
                    sp.dma_start(dst, xn[:, p] if p < 2 else x[:, t]).then_inc(y_out, 16)
                else:
                    sp.dma_start(dst[:, 0:D // 2], x[:, t, 0:D // 2]).then_inc(y_out, 16)
                    sp.wait_ge(xn_ready.sem, xn_ready.at(DEPTH, NT + 1))
                    sp.dma_start(dst[:, D // 2:], x[:, t, D // 2:]).then_inc(y_out, 16)
            sp.wait_ge(y_out, 16 * (NT + 1))

        @block.tensor
        def _(pe):
            three = ((0, 0), (0, 1), (1, 0))
            norms, inners, ws = (norm_hi, norm_lo), (inner_hi, inner_lo), (w_hi, w_lo)

            pe.sem_inc(group_done.sem, 1)
            pe.wait_ge(x_in[SAMPLE], 16)
            for _ in range(WARMING):
                pe.matmul(small_bank[2][:, 0:P], x[:, SAMPLE, 0:P], x[:, SAMPLE, 0:P], start=True, stop=True)
            pe.wait_ge(identity_in, 16)

            def wait_unit(layer, chunk, half, piece=PIECES - 1):
                pe.wait_ge(w_hi_ready.sem, w_hi_ready.at(layer, made(chunk, half, piece)))
                pe.wait_ge(w_lo_ready.sem, w_lo_ready.at(layer, made(chunk, half, piece)))

            def tokens_product(out, tile, act, k_of, w_of, before=None):
                ks = k_of
                for n, k in enumerate(ks):
                    if before:
                        before(n)
                    for m, (a, b) in enumerate(three):
                        mm = pe.matmul(out, act[a][:, k, tile * P:(tile + 1) * P], w_of(b, n),
                                       start=(n == 0 and m == 0), stop=(n == len(ks) - 1 and m == 2))
                return mm

            def features_product(out, ft, half, par, before=None):
                for k in range(KT):
                    if before:
                        before(k)
                    for m, (a, b) in enumerate(three):
                        mm = pe.matmul(out, ws[a][:, par, k // 4, k % 4, ft * P:(ft + 1) * P],
                                       norms[b][:, k, half * HALF:(half + 1) * HALF],
                                       start=(k == 0 and m == 0), stop=(k == KT - 1 and m == 2))
                return mm

            def turn(layer, what):
                n = TURN[what]
                if n >= 2:
                    pe.wait_ge(turn_read.sem, turn_read.at(layer, n - 1))
                    if n - 2 in SPLIT_TURNS:
                        pe.wait_ge(turn_lo.sem, turn_lo.at(layer, split_turns_to(n - 2)))
                out = turn_bank[n % 2]
                kind = what[0]
                if kind in ("n1", "n2"):
                    p, c = what[1:]
                    if c == 0:
                        pe.wait_ge(xn_ready.sem, xn_ready.at(layer, NT * (kind == "n2") + p + 1))
                    src = [xn[:, p % 2, (4 * c + i) * P:(4 * c + i + 1) * P] for i in range(4)]
                elif kind == "k":
                    pe.wait_ge(k_rotated.sem, k_rotated.at(layer, what[1] + 1))
                    src = [k_rot[:, ORDER[what[1]], i * P:(i + 1) * P] for i in range(4)]
                elif kind == "q":
                    pe.wait_ge(q_rotated.sem, q_rotated.at(layer, what[1] + 1))
                    src = [q_rot[:, what[1] % 2, i * P:(i + 1) * P] for i in range(4)]
                elif kind == "o":
                    pe.wait_ge(o_gated.sem, o_gated.at(layer, what[1] + 1))
                    src = [o[:, what[1], i * P:(i + 1) * P] for i in range(4)]
                if kind == "past":
                    pe.wait_ge(past_in.sem, past_in.at(layer, 16))
                    settle(pe)
                    for i in range(FT):
                        mm = pe.transpose(out[:, i * 2 * NB:(i + 1) * 2 * NB], conv_rows[0:2 * NB, i * P:(i + 1) * P],
                                          identity[0:2 * NB, 0:2 * NB])
                elif kind == "tail":
                    pe.wait_ge(tail_ready.sem, tail_ready.at(layer, 1))
                    for i in range(FT):
                        mm = pe.transpose(out[0:2 + 2 * NB, i * P:(i + 1) * P], tail[:, i], identity)
                else:
                    for i in range(4):
                        mm = pe.transpose(out[:, i * P:(i + 1) * P], src[i], identity)
                mm.then_inc(turned.sem, 1)

            def small(layer, what):
                n = SMALL[what]
                out = small_bank[n % 3]
                kind, p = what
                needs = [n - 2]
                if kind == "Y":
                    needs += [SMALL["S", p] + 1] + ([SMALL["R", p - 1] + 1] if p >= 2 else [])
                if kind == "so":
                    needs += [SMALL["S", 0] + 1]
                if max(needs) >= 1:
                    pe.wait_ge(small_read.sem, small_read.at(layer, max(needs)))
                if kind == "S":
                    pe.wait_ge(turn_read.sem, turn_read.at(layer, TURN["q", p] + 1))
                    for h in range(H):
                        qT = qT_s[:, h] if p == 0 else qT_p[:, p % 2, h]
                        mm = pe.matmul(out[:, h * P:(h + 1) * P], kT[:, ORDER[p], h], qT, start=True, stop=True)
                elif kind == "R":
                    pe.wait_ge(k_decayed.sem, k_decayed.at(layer, p + 1))
                    for h in range(H):
                        mm = pe.matmul(out[:, h * HD:(h + 1) * HD], k_rot[:, ORDER[p], h * HD:(h + 1) * HD],
                                       v[:, ORDER[p], h * HD:(h + 1) * HD], start=True, stop=True)
                elif kind == "Y":
                    for h in range(H):
                        cols = out[:, h * HD:(h + 1) * HD]
                        mm = pe.matmul(cols, scores_p[:, h], v[:, ORDER[p], h * HD:(h + 1) * HD],
                                       start=True, stop=(p == 1))
                        if p >= 2:
                            mm = pe.matmul(cols, qT_p[:, p % 2, h], ret_state[:, h], start=False, stop=True)
                elif kind == "so":
                    h = p
                    pe.wait_ge(q_spread_ready.sem, q_spread_ready.at(layer, h + 1))
                    pe.wait_ge(state_in[h % 2].sem, state_in[h % 2].at(layer, 16 * (h // 2 + 1)))
                    pe.matmul(out[:, 0:HD], scores_s[:, h], v[:, SAMPLE, h * HD:(h + 1) * HD], start=True, stop=False)
                    for b in range(NB):
                        mm = pe.matmul(out[:, 0:HD], q_spread[:, b], past_state[h % 2][:, b],
                                       start=False, stop=(b == NB - 1))
                else:
                    h, c = p, int(kind == "sb")
                    pe.wait_ge(v_spread_ready.sem, v_spread_ready.at(layer, h + 1))
                    if (h, c) == (0, 0):
                        pe.wait_ge(k_decayed.sem, k_decayed.at(layer, 1))
                    mm = pe.matmul(out[:], k_rot[:, SAMPLE, h * HD:(h + 1) * HD], v_spread[:, 4 * c:4 * c + 4],
                                   start=True, stop=True)
                mm.then_inc(small_done.sem, 1)

            for c in range(2):
                turn(0, ("n1", 0, c))
            with pe.Fori(0, DEPTH) as layer:
                for n, g in enumerate(GROUPS):
                    stage, chunk = g[0], max(c for c in range(MIX_CHUNKS) if STAGE_START[c] <= n)
                    par, out = chunk % 2, mix_bank[n % 3]
                    if n >= 3:
                        if n - 3 in MIX_SCALAR:
                            pe.wait_ge(scalar_read.sem, scalar_read.at(layer, MIX_SCALAR.index(n - 3) + 1))
                        else:
                            pe.wait_ge(vector_read.sem, vector_read.at(layer, MIX_VECTOR.index(n - 3) + 1))
                    if stage == "K":
                        last = TURN["n1", g[1], 1]
                        pe.wait_ge(turn_read.sem, turn_read.at(layer, last + 1))
                        pe.wait_ge(turn_lo.sem, turn_lo.at(layer, split_turns_to(last)))

                    def weights_there(k, first=(n == STAGE_START[chunk]), chunk=chunk, stage=stage):
                        if stage == "K" and k == KT // 2 and g[1] + 1 < NT:
                            for c in range(2):
                                turn(layer, ("n1", g[1] + 1, c))
                        if first and chunk == 0:
                            wait_unit(layer, chunk, k // 4, k % 4)
                        elif first and k % 4 == 0:
                            wait_unit(layer, chunk, k // 4)
                        if first and chunk == 7:
                            if k == 0:
                                pe.wait_ge(turn_read.sem, turn_read.at(layer, TURN["o", NT - 1] + 1))
                                pe.wait_ge(turn_lo.sem, turn_lo.at(layer, split_turns_to(TURN["o", NT - 1])))
                            if k >= FT:
                                pe.wait_ge(mix_hi.sem, mix_hi.at(layer, 2 * (k - FT + 1)))
                                pe.wait_ge(mix_lo.sem, mix_lo.at(layer, 2 * (k - FT + 1)))

                    if stage in "KVQGO":
                        tile = {"O": g[-1], "G": g[1]}.get(stage, ORDER[g[1]] if stage in "KVQ" else None)
                        act = inners if stage == "O" else norms
                        mm = tokens_product(out[:], tile, act, range(KT),
                                            lambda b, k: ws[b][:, par, k // 4, k % 4], weights_there)
                    else:
                        mm = features_product(out[:, 0:HALF], g[1], g[2], par, weights_there)
                    mm.then_inc(group_done.sem, 1)
                    for s in GAPS.get(g, []):
                        small(layer, s)
                    for s in TURN_AFTER.get(g, []):
                        turn(layer, s)

                def up_block(b):
                    first = isinstance(b, int) and b == 0
                    par, start = parity_up(first), 0 if first else UPS
                    for j in range(UPS):
                        half, ft = divmod(j, FT)
                        if first and j < 3:
                            pe.wait_ge(vector_read.sem, vector_read.at(layer, len(MIX_VECTOR) - 2 + j))
                        if not first and j < 6:
                            pe.wait_ge(vector_read.sem, vector_read.at(
                                layer, b * DOWNS + (len(MIX_VECTOR) - DOWNS - 5 + j)))
                        if not (first and j < 6):
                            pe.wait_ge(scalar_read.sem, scalar_read.at(layer, b * UPS + (len(MIX_SCALAR) - 5 + j)))
                        if first and ft == 0:
                            last = TURN["n2", 2 if half == 0 else NT - 1, 1]
                            pe.wait_ge(turn_read.sem, turn_read.at(layer, last + 1))
                            pe.wait_ge(turn_lo.sem, turn_lo.at(layer, split_turns_to(last)))

                        def weights_there(k, j=j):
                            if j == 0 and k % 4 == 0:
                                wait_unit(layer, up_chunk(b), k // 4)

                        mm = features_product(mlp_bank[(start + j) % 6][:, 0:HALF], ft, half, par, weights_there)
                        mm.then_inc(group_done.sem, 1)
                        if first and j == 1:
                            turn(layer, ("n2", NT - 1, 0))
                            turn(layer, ("n2", NT - 1, 1))

                def down_block(d, buf):
                    last = isinstance(d, int) and d == NBLK - 1
                    par = parity_down(last)
                    start = (PER_LAYER - MIX - DOWNS) if last else 2 * UPS
                    for j in range(DOWNS):
                        dh, p = divmod(j, NT)
                        if j < 6 and not last:
                            pe.wait_ge(scalar_read.sem, scalar_read.at(
                                layer, d * UPS + (len(MIX_SCALAR) + UPS + 3 + j)))
                        else:
                            pe.wait_ge(vector_read.sem, vector_read.at(
                                layer, d * DOWNS + (len(MIX_VECTOR) - 5 + j)))
                        if j == 0:
                            pe.wait_ge(hidden_hi.sem, hidden_hi.at(layer, d * UPS + UPS))
                            pe.wait_ge(hidden_lo.sem, hidden_lo.at(layer, d * UPS + UPS))
                        if p == 0:
                            wait_unit(layer, down_chunk(d), dh)
                        mm = tokens_product(mlp_bank[(start + j) % 6][:], ORDER[p], inners,
                                            range(buf * FT, buf * FT + FT),
                                            lambda b, k: ws[b][:, par, dh, k])
                        mm.then_inc(group_done.sem, 1)
                        if last and dh == 1 and p == 2:
                            with pe.If(layer < DEPTH - 1):
                                for c in range(2):
                                    turn(layer + 1, ("n1", 0, c))

                up_block(0)
                with pe.Fori(0, NBLK // 2 - 1) as turn_i:
                    for b in range(2):
                        up_block(turn_i * 2 + (b + 1))
                        down_block(turn_i * 2 + b, b)
                up_block(NBLK - 1)
                down_block(NBLK - 2, 0)
                down_block(NBLK - 1, 1)

        @block.scalar
        def _(act):
            def split_unit(layer, chunk, half, par, groups_before):
                act.wait_ge(raw_in[half].sem, raw_in[half].at(layer, (chunk + 1) * 16))
                act.wait_ge(group_done.sem, group_done.at(layer, groups_before))
                nc.scalar.activation(w_hi[:, par, half], w_raw[:, half], ACT.Copy).then_inc(w_hi_ready.sem, 1)

            def split_first(layer, half):
                act.wait_ge(raw_in[half].sem, raw_in[half].at(layer, 16))
                for k in range(PIECES):
                    nc.scalar.activation(w_hi[:, 0, half, k], w_raw[:, half, k], ACT.Copy
                                         ).then_inc(w_hi_ready.sem, 1)

            def split_chunk(layer, chunk, par, groups_before):
                for half in range(2):
                    split_unit(layer, chunk, half, par, groups_before)

            def square(layer, base, p, tile):
                if p >= 2:
                    turns = TURN["n1" if base == 0 else "n2", p - 2, 1]
                    act.wait_ge(turned.sem, turned.at(layer, turns + 1))
                nc.scalar.activation(xn[:, p % 2], x[:, tile], ACT.Square,
                                     accum_out=sums[:, p:p + 1]).then_inc(squares.sem, 1)

            def read_turn(layer, what):
                n = TURN[what]
                src, kind = turn_bank[n % 2], what[0]
                act.wait_ge(turned.sem, turned.at(layer, n + 1))
                if kind in ("n1", "n2"):
                    p, c = what[1:]
                    tile = ORDER[p] if kind == "n1" else p
                    dst = norm_hi[:, 4 * c:4 * c + 4, tile * P:(tile + 1) * P]
                    src = src[:].rearrange("p (k t) -> p k t", k=4)
                elif kind == "k":
                    dst, src = kT[:, ORDER[what[1]]].rearrange("p h t -> p (h t)"), src[:]
                elif kind == "q":
                    q = qT_s[:] if what[1] == 0 else qT_p[:, what[1] % 2]
                    dst, src = q.rearrange("p h t -> p (h t)"), src[:]
                elif kind == "o":
                    dst = inner_hi[:, 0:FT, what[1] * P:(what[1] + 1) * P]
                    src = src[:].rearrange("p (k t) -> p k t", k=4)
                elif kind == "past":
                    for ft in range(FT):
                        to = u[:, ft, SEQ + 2:UPAD].rearrange("p (b s) -> p b s", b=NB)[:, :, 0:2]
                        of = src[:, ft * 2 * NB:(ft + 1) * 2 * NB].rearrange("p (b r) -> p b r", b=NB)
                        ins = nc.scalar.activation(to, of, ACT.Copy)
                    ins.then_inc(turn_read.sem, 1)
                    return
                else:
                    dst, src = conv_rows[0:2 + 2 * NB, :], src[0:2 + 2 * NB, :]
                nc.scalar.activation(dst, src, ACT.Copy).then_inc(turn_read.sem, 1)

            act.dma_start(identity, consts[:, 0:P]).then_inc(identity_in, 16)

            def square1(layer, p):
                act.wait_ge(x_in[ORDER[p]], 16)
                act.wait_ge(vector_read.sem, vector_read.at(layer, 0))
                square(layer, 0, p, ORDER[p])

            act.wait_ge(x_in[ORDER[0]], 16)
            square(0, 0, 0, ORDER[0])
            for c in range(2):
                read_turn(0, ("n1", 0, c))
            split_first(0, 0)
            act.wait_ge(x_in[ORDER[1]], 16)
            square(0, 0, 1, ORDER[1])

            with act.Fori(0, DEPTH) as layer:
                act.wait_ge(group_done.sem, group_done.at(layer, 0))
                split_first(layer, 1)
                for c in range(2):
                    read_turn(layer, ("n1", 1, c))
                for p in range(2, NT):
                    square1(layer, p)
                    if p == NT - 1:
                        split_unit(layer, 1, 0, 1, 0)
                    for c in range(2):
                        read_turn(layer, ("n1", p, c))
                split_unit(layer, 1, 1, 1, 0)

                split_chunk(layer, 2, 0, STAGE_START[1])
                for p in range(NT):
                    n = GROUP["V", p]
                    act.wait_ge(group_done.sem, group_done.at(layer, n + 1))
                    nc.scalar.activation(v[:, ORDER[p]], mix_bank[n % 3][:], ACT.Copy).then_inc(scalar_read.sem, 1)
                    read_turn(layer, ("k", p))

                split_chunk(layer, 3, 1, STAGE_START[2])
                for p in range(4):
                    if p == 3:
                        act.wait_ge(small_done.sem, small_done.at(layer, SMALL["Y", 1] + 1))
                    read_turn(layer, ("q", p))

                split_chunk(layer, 4, 0, STAGE_START[3])
                for t in range(NT):
                    n = GROUP["G", t]
                    act.wait_ge(group_done.sem, group_done.at(layer, n + 1))
                    if t >= 2:
                        act.wait_ge(o_gated.sem, o_gated.at(layer, t - 1))
                    nc.scalar.activation(gate[:, (t + 1) % 2], mix_bank[n % 3][:], ACT.Sigmoid
                                         ).then_inc(sigmoid_ready.sem, 1)
                    if t == 0:
                        act.wait_ge(small_done.sem, small_done.at(layer, SMALL["Y", 2] + 1))
                        read_turn(layer, ("q", 4))
                    if t == 3:
                        act.wait_ge(small_read.sem, small_read.at(layer, len(SMALLS)))
                        for s in range(2):
                            read_turn(layer, ("o", s))
                for s in range(2, 4):
                    read_turn(layer, ("o", s))

                split_chunk(layer, 5, 1, STAGE_START[4])
                read_turn(layer, ("o", 4))
                read_turn(layer, ("past",))
                for ft in range(FT):
                    for half in range(2):
                        n = GROUP["C", ft, half]
                        act.wait_ge(group_done.sem, group_done.at(layer, n + 1))
                        src = mix_bank[n % 3]
                        if half == 0:
                            ins = nc.scalar.activation(u[:, ft, 2:2 + HALF], src[:, 0:HALF], ACT.Copy)
                        else:
                            rest = SEQ - HALF
                            nc.scalar.activation(u[:, ft, 2 + HALF:2 + SEQ], src[:, 0:rest], ACT.Copy)
                            ins = nc.scalar.activation(u_sample(ft, 2), sample_cols(src[:, rest:HALF]), ACT.Copy)
                        ins.then_inc(scalar_read.sem, 1)

                split_chunk(layer, 6, 0, STAGE_START[5])

                def first_tap(ft):
                    if ft < 2:
                        act.wait_ge(vector_read.sem, vector_read.at(
                            layer, MIX_VECTOR.index(GROUP["H", ft, 1]) + 1))
                        if ft == 0:
                            act.wait_ge(layer_rows_in.sem, layer_rows_in.at(layer, 32))
                    else:
                        act.wait_ge(vector_read.sem, vector_read.at(
                            layer, MIX_VECTOR.index(GROUP["H", ft, 1]) + 1))
                        act.wait_ge(mix_lo.sem, mix_lo.at(layer, 2 * (ft - 1)))
                    nc.scalar.activation(z[:, ft % 2, 0:SEQ], u[:, ft, 0:SEQ], ACT.Copy,
                                         scale=conv_taps[:, ft, 0:1])
                    nc.scalar.activation(sample_cols(z[:, ft % 2, SEQ:TOK]), u_sample(ft, 0), ACT.Copy,
                                         scale=conv_taps[:, ft, 0:1]).then_inc(tap0_ready.sem, 1)

                first_tap(0)
                first_tap(1)
                split_chunk(layer, 7, 1, STAGE_START[6])
                read_turn(layer, ("tail",))
                for ft in range(FT):
                    for half in range(2):
                        act.wait_ge(vector_read.sem, vector_read.at(
                            layer, MIX_VECTOR.index(GROUP["B", ft, half]) + 1))
                        cols = slice(half * HALF, (half + 1) * HALF)
                        nc.scalar.activation(inner_hi[:, FT + ft, cols], z[:, ft % 2, cols], ACT.Copy
                                             ).then_inc(mix_hi.sem, 1)
                    if ft + 2 < FT:
                        first_tap(ft + 2)

                split_chunk(layer, 8, 0, STAGE_START[7])
                split_chunk(layer, 9, 1, STAGE_START[8])
                for t in range(NT):
                    act.wait_ge(vector_read.sem, vector_read.at(
                        layer, MIX_VECTOR.index(GROUP["O", 1, t]) + 1))
                    square(layer, NT, t, t)
                    if t >= 1:
                        for c in range(2):
                            read_turn(layer, ("n2", t - 1, c))

                def up_block(b, buf, chunk, par, before):
                    split_chunk(layer, chunk, par, before)

                    def hi_part(j):
                        half, ft = divmod(j, FT)
                        act.wait_ge(squared.sem, squared.at(layer, b * UPS + (j + 1)))
                        nc.scalar.activation(inner_hi[:, buf * FT + ft, half * HALF:(half + 1) * HALF],
                                             relu[:, j % 4], ACT.Copy).then_inc(hidden_hi.sem, 1)

                    first = isinstance(b, int) and b == 0
                    for j in range(UPS):
                        act.wait_ge(group_done.sem, group_done.at(layer, up_group(b, j + 1)))
                        if not (first and j < 4):
                            act.wait_ge(hidden_lo.sem, hidden_lo.at(layer, b * UPS + (j - 3)))
                        slot = (0 if first else UPS) + j
                        nc.scalar.activation(relu[:, j % 4], mlp_bank[slot % 6][:, 0:HALF], ACT.Relu
                                             ).then_inc(scalar_read.sem, 1)
                        if j >= 1:
                            hi_part(j - 1)
                    hi_part(UPS - 1)

                for c in range(2):
                    read_turn(layer, ("n2", NT - 1, c))
                up_block(0, 0, 10, 0, up_group(0, 0))
                with act.Fori(0, NBLK // 2 - 1) as i:
                    for b in range(2):
                        up, down = i * 2 + (b + 1), i * 2 + b
                        up_block(up, (b + 1) % 2, down_chunk(down), 1, up_group(up, 0))
                        split_chunk(layer, up_chunk(i * 2 + (b + 2)), 0, down_group(down, 0))
                up_block(NBLK - 1, 1, down_chunk(NBLK - 2), 1, up_group(NBLK - 1, 0))
                split_chunk(layer, down_chunk(NBLK - 1), 0, down_group(NBLK - 2, 0))
                with act.If(layer < DEPTH - 1):
                    act.wait_ge(group_done.sem, group_done.at(layer, PER_LAYER - NT))
                    split_first(layer + 1, 0)
                for p in range(2):
                    act.wait_ge(vector_read.sem, vector_read.at(layer, VECTOR_PER_LAYER - NT + p + 1))
                    square(layer + 1, 0, p, ORDER[p])
                with act.If(layer < DEPTH - 1):
                    for c in range(2):
                        read_turn(layer + 1, ("n1", 0, c))

            for p in range(2, NT):
                act.wait_ge(vector_read.sem, vector_read.at(DEPTH - 1, VECTOR_PER_LAYER - NT + p + 1))
                nc.scalar.activation(squares_out[:, p % 2], x[:, ORDER[p]], ACT.Square,
                                     accum_out=sums[:, p:p + 1]).then_inc(squares.sem, 1)

        @block.gpsimd
        def _(pool):
            nc.gpsimd.memset(minus_half[:], -0.5).then_inc(half_ready, 1)
            pool.wait_ge(half_ready, 1)

            eps_n, turn_of = [0], [0]

            def rstd_of(out, tmp, src, scale, eps, done):
                settle(pool)
                nc.gpsimd.tensor_scalar(tmp, src, scale, eps, ALU.mult, ALU.add).then_inc(eps_step.sem, 1)
                eps_n[0] += 1
                pool.wait_ge(eps_step.sem, eps_step.at(turn_of[0], eps_n[0]))
                nc.gpsimd.tensor_tensor(out, tmp, minus_half[:, 0:tmp.shape[1]], ALU.pow).then_inc(done.sem, 1)

            def row_rstd(layer, base, p):
                pool.wait_ge(squares.sem, squares.at(layer, base + p + 1))
                rstd_of(rstd[:, p:p + 1], var[:, p:p + 1], sums[:, p:p + 1], 1.0 / D, LN_EPS, rstd_ready)

            def rotate(layer, stage, p, dst, done):
                pool.wait_ge(vector_read.sem, vector_read.at(layer, MIX_VECTOR.index(GROUP[stage, p]) + 1))
                a = dst.rearrange("p (h c f) -> p h c f", h=H, c=2)
                b = rope_tmp[:].rearrange("p (h c f) -> p h c f", h=H, c=2)
                nc.gpsimd.tensor_tensor(a[:, :, 0], a[:, :, 0], b[:, :, 1], ALU.subtract)
                nc.gpsimd.tensor_tensor(a[:, :, 1], a[:, :, 1], b[:, :, 0], ALU.add).then_inc(done.sem, 1)

            def decay_k(layer, p):
                if p == 0:
                    pool.wait_ge(consts_in, 16)
                pool.wait_ge(turned.sem, turned.at(layer, TURN["k", p] + 1))
                kk = k_rot[:, ORDER[p]].rearrange("p (h f) -> p h f", h=H)
                nc.gpsimd.tensor_tensor(kk, kk, k_decay[:, int(p == 0)].unsqueeze(2).to_broadcast([P, H, HD]),
                                        ALU.mult).then_inc(k_decayed.sem, 1)

            def spread_q(layer, h):
                pool.wait_ge(turn_read.sem, turn_read.at(layer, TURN["q", 0] + 1))
                if h == 0:
                    pool.wait_ge(spread_zero.sem, spread_zero.at(layer, 1))
                else:
                    pool.wait_ge(small_done.sem, small_done.at(layer, SMALL["so", h - 1] + 1))
                settle(pool)
                ins = nc.gpsimd.tensor_copy(diagonal_blocks(q_spread), sample_cols(qT_s[:, h]))
                ins.then_inc(q_spread_ready.sem, 1)

            def spread_v(layer, h):
                if h >= 1:
                    pool.wait_ge(small_done.sem, small_done.at(layer, SMALL["sb", h - 1] + 1))
                vv = v[:, SAMPLE, h * HD:(h + 1) * HD]
                nc.gpsimd.tensor_tensor(v_spread[:], vv.unsqueeze(1).to_broadcast([P, NB, HD]),
                                        stream_of.unsqueeze(2).to_broadcast([P, NB, HD]), ALU.mult
                                        ).then_inc(v_spread_ready.sem, 1)

            def diagonal_blocks(t):
                a = t[:].rearrange("p b t -> p (b t)")
                a = a[:, 0:NB * (P + NS)] if NB * (P + NS) <= NB * P else a
                return bass.AP(tensor=a.tensor, offset=a.offset, ap=[list(a.ap[0]), [P + NS, NB], [1, NS]])

            def finish_o(layer, p):
                pool.wait_ge(o_normed.sem, o_normed.at(layer, STAT[p] + 1))
                if STAT[p] == 0:
                    pool.wait_ge(layer_rows_in.sem, layer_rows_in.at(layer, 32))
                oo = o[:, ORDER[p]]
                nc.gpsimd.tensor_tensor(oo, oo, ret_row[:], ALU.mult).then_inc(o_scaled.sem, 1)

            def group_norm(layer, p):
                pool.wait_ge(group_stats.sem, group_stats.at(layer, STAT[p] + 1))
                rstd_of(group_rstd[:], group_var[:], group_mv[:, :, 1], 1.0, GN_EPS, group_rstd_ready)

            def serve_streams(layer, h):
                spread_q(layer, h)
                spread_v(layer, h)

            eps_n[0] = -2
            row_rstd(0, 0, 0)
            row_rstd(0, 0, 1)
            with pool.Fori(0, DEPTH) as layer:
                eps_n[0], turn_of[0] = 0, layer
                pool.wait_ge(group_done.sem, group_done.at(layer, 0))
                settle(pool)
                nc.gpsimd.memset(q_spread[:], 0.0).then_inc(spread_zero.sem, 1)
                for p in range(NT):
                    if p + 2 < NT:
                        row_rstd(layer, 0, p + 2)
                    rotate(layer, "K", p, k_rot[:, ORDER[p]], k_rotated)
                for p in range(NT):
                    decay_k(layer, p)
                pool.wait_ge(scalar_read.sem, scalar_read.at(layer, 1))
                spread_v(layer, 0)
                for p in range(NT):
                    if p == 2:
                        spread_q(layer, 0)
                    if p == 4:
                        serve_streams(layer, 1)
                    rotate(layer, "Q", p, q_rot[:, p % 2], q_rotated)
                serve_streams(layer, 2)
                group_norm(layer, 1)
                finish_o(layer, 1)
                serve_streams(layer, 3)
                for p in (2, 3, 0, 4):
                    group_norm(layer, p)
                    finish_o(layer, p)
                for t in range(NT):
                    row_rstd(layer, NT, t)
                for p in range(2):
                    row_rstd(layer + 1, 0, p)
                assert eps_n[0] == eps_step.per_layer
            eps_n[0], turn_of[0] = 0, DEPTH
            for p in range(2, NT):
                row_rstd(DEPTH, 0, p)

        @block.vector
        def _(dve):
            dve.sem_inc(vector_read.sem, 1)
            f = lambda t: t.bitcast(f32)

            def split_unit(layer, chunk, half, par, part=None):
                ks = slice(0, 4) if part is None else slice(2 * part, 2 * part + 2)
                if part != 1:
                    dve.wait_ge(w_hi_ready.sem, w_hi_ready.at(layer, made(chunk, half)))
                ins = nc.vector.tensor_tensor(w_lo[:, par, half, ks], w_raw[:, half, ks], f(w_hi[:, par, half, ks]),
                                              ALU.subtract)
                if part != 0:
                    ins.then_inc(w_lo_ready.sem, 1)

            def split_first(layer, half):
                for k in range(PIECES):
                    dve.wait_ge(w_hi_ready.sem, w_hi_ready.at(layer, made(0, half, k)))
                    nc.vector.tensor_tensor(w_lo[:, 0, half, k], w_raw[:, half, k], f(w_hi[:, 0, half, k]),
                                            ALU.subtract).then_inc(w_lo_ready.sem, 1)

            def split_chunk(layer, chunk, par):
                for half in range(2):
                    split_unit(layer, chunk, half, par)

            def normalise(layer, base, p, tile, row_count):
                dve.wait_ge(rstd_ready.sem, rstd_ready.at(layer, base + p + 1))
                dve.wait_ge(norm_row_in.sem, norm_row_in.at(layer, row_count))
                nc.vector.scalar_tensor_tensor(out=xn[:, p % 2], in0=x[:, tile], scalar=rstd[:, p:p + 1],
                                               in1=norm_row[:], op0=ALU.mult, op1=ALU.mult).then_inc(xn_ready.sem, 1)

            def normalise_last(p, pieces=1):
                dve.wait_ge(rstd_ready.sem, rstd_ready.at(DEPTH, p + 1))
                dve.wait_ge(norm_row_in.sem, norm_row_in.at(DEPTH, 16))
                for i in range(pieces):
                    cols = slice(i * D // pieces, (i + 1) * D // pieces)
                    xx = x[:, ORDER[p], cols]
                    nc.vector.scalar_tensor_tensor(out=xx, in0=xx, scalar=rstd[:, p:p + 1], in1=norm_row[:, cols],
                                                   op0=ALU.mult, op1=ALU.mult).then_inc(xn_ready.sem, 1)

            def read_turn_lo(layer, what):
                n = TURN[what]
                src = turn_bank[n % 2][:].rearrange("p (k t) -> p k t", k=4)
                if what[0] == "o":
                    ks, tile, hi, lo = slice(0, FT), what[1], inner_hi, inner_lo
                else:
                    p, c = what[1:]
                    ks, tile = slice(4 * c, 4 * c + 4), ORDER[p] if what[0] == "n1" else p
                    hi, lo = norm_hi, norm_lo
                cols = slice(tile * P, (tile + 1) * P)
                dve.wait_ge(turn_read.sem, turn_read.at(layer, n + 1))
                nc.vector.tensor_tensor(lo[:, ks, cols], src, f(hi[:, ks, cols]), ALU.subtract
                                        ).then_inc(turn_lo.sem, 1)

            def wait_group(layer, n):
                dve.wait_ge(group_done.sem, group_done.at(layer, n + 1))

            def rope(layer, stage, p, dst, done):
                n = GROUP[stage, p]
                src = mix_bank[n % 3][:].rearrange("p (h f) -> p h f", f=HD // 2)
                wait_group(layer, n)
                if (stage, p) == ("K", 0):
                    dve.wait_ge(consts_in, 16)
                if stage == "Q" and p >= 2:
                    dve.wait_ge(turned.sem, turned.at(layer, TURN["q", p - 2] + 1))
                tab = [cos_sin[:, ORDER[p], c].unsqueeze(1).to_broadcast([P, 2 * H, HD // 2]) for c in range(2)]
                nc.vector.tensor_tensor(dst.rearrange("p (h f) -> p h f", f=HD // 2), src, tab[0], ALU.mult)
                if (stage, p) != ("K", 0):
                    prev = done.at(layer, p) if p else k_rotated.at(layer, NT)
                    dve.wait_ge((done if p else k_rotated).sem, prev)
                nc.vector.tensor_tensor(rope_tmp[:].rearrange("p (h f) -> p h f", f=HD // 2), src, tab[1], ALU.mult
                                        ).then_inc(vector_read.sem, 1)

            def stats(layer, p):
                tile = ORDER[p]
                last = SMALL["so", H - 1] if p == 0 else SMALL["Y", p]
                dve.wait_ge(small_read.sem, small_read.at(layer, last + 1))
                if STAT[p] >= 1:
                    dve.wait_ge(o_normed.sem, o_normed.at(layer, STAT[p]))
                for h in range(H):
                    ins = nc.vector.bn_stats(group_parts[:, h], o[:, tile, h * HD:(h + 1) * HD])
                ins.then_inc(stats_step.sem, 1)
                dve.wait_ge(stats_step.sem, stats_step.at(layer, STAT[p] + 1))
                settle(dve)
                for h in range(H):
                    ins = nc.vector.bn_aggr(group_mv[:, h], group_parts[:, h])
                ins.then_inc(group_stats.sem, 1)

            def norm_heads(layer, p):
                dve.wait_ge(group_rstd_ready.sem, group_rstd_ready.at(layer, STAT[p] + 1))
                for h in range(H):
                    oo = o[:, ORDER[p], h * HD:(h + 1) * HD]
                    ins = nc.vector.tensor_scalar(oo, oo, group_mv[:, h, 0:1], group_rstd[:, h:h + 1],
                                                  ALU.subtract, ALU.mult)
                ins.then_inc(o_normed.sem, 1)

            def read_small(layer, what):
                n = SMALL[what]
                kind, p = what
                src = small_bank[n % 3]
                last = SMALL["R", p] if kind == "Y" else n
                dve.wait_ge(small_done.sem, small_done.at(layer, last + 1))
                if kind == "S":
                    dst, mask = (scores_s, mask_s) if p == 0 else (scores_p, mask_p)
                    ins = nc.vector.tensor_tensor(dst[:].rearrange("p h t -> p (h t)"), src[:], mask, ALU.mult)
                elif kind == "R":
                    if p == 1:
                        ins = nc.vector.tensor_copy(ret_state[:].rearrange("p h f -> p (h f)"), src[:])
                    else:
                        dve.wait_ge(small_read.sem, small_read.at(layer, SMALL["R", p - 1] + 1))
                        for h in range(H):
                            ins = nc.vector.scalar_tensor_tensor(
                                out=ret_state[:, h], in0=ret_state[:, h], scalar=gamma[h] ** P,
                                in1=src[:, h * HD:(h + 1) * HD], op0=ALU.mult, op1=ALU.add)
                elif kind == "Y":
                    ins = nc.vector.tensor_tensor(
                        o[:, ORDER[p]].rearrange("p (h f) -> p h f", h=H), src[:].rearrange("p (h f) -> p h f", h=H),
                        q_decay[:, 0].unsqueeze(2).to_broadcast([P, H, HD]), ALU.mult)
                elif kind == "so":
                    dve.wait_ge(v_spread_ready.sem, v_spread_ready.at(layer, p + 1))
                    ins = nc.vector.tensor_scalar(o[:, SAMPLE, p * HD:(p + 1) * HD], src[:, 0:HD],
                                                  q_decay[:, 1, p:p + 1], None, ALU.mult)
                else:
                    h, c = p, int(kind == "sb")
                    if c == 0:
                        dve.wait_ge(state_in[h % 2].sem, state_in[h % 2].at(layer, 16 * (h // 2 + 1)))
                    st = past_state[h % 2][:, 4 * c:4 * c + 4].rearrange("p b f -> p (b f)")
                    ins = nc.vector.scalar_tensor_tensor(out=st, in0=st, scalar=gamma[h] ** NS, in1=src[:],
                                                         op0=ALU.mult, op1=ALU.add)
                ins.then_inc(small_read.sem, 1)

            def gate_o(layer, t):
                n = GROUP["G", t]
                dve.wait_ge(sigmoid_ready.sem, sigmoid_ready.at(layer, t + 1))
                gg = gate[:, (t + 1) % 2]
                nc.vector.tensor_tensor(gg, gg, mix_bank[n % 3][:], ALU.mult).then_inc(vector_read.sem, 1)

            def finish_gate(layer, t):
                dve.wait_ge(vector_read.sem, vector_read.at(layer, MIX_VECTOR.index(GROUP["G", t]) + 1))
                dve.wait_ge(o_scaled.sem, o_scaled.at(layer, STAT[ORDER.index(t)] + 1))
                nc.vector.tensor_tensor(o[:, t], o[:, t], gate[:, (t + 1) % 2], ALU.mult).then_inc(o_gated.sem, 1)

            normalise(0, 0, 0, ORDER[0], 16)
            for c in range(2):
                read_turn_lo(0, ("n1", 0, c))
            split_first(0, 0)
            normalise(0, 0, 1, ORDER[1], 16)
            with dve.Fori(0, DEPTH) as layer:
                split_first(layer, 1)
                for p in range(NT):
                    if p + 1 < NT:
                        for c in range(2):
                            read_turn_lo(layer, ("n1", p + 1, c))
                    if p + 2 < NT:
                        normalise(layer, 0, p + 2, ORDER[p + 2], 16)
                    rope(layer, "K", p, k_rot[:, ORDER[p]], k_rotated)
                    if p in (2, 3):
                        split_unit(layer, 1, p - 2, 1)

                split_chunk(layer, 2, 0)

                for p in range(NT):
                    rope(layer, "Q", p, q_rot[:, p % 2], q_rotated)
                    if p < 2:
                        split_unit(layer, 3, p, 1)
                    for s in GAPS.get(("Q", p), []):
                        read_small(layer, s)
                stats(layer, 1)
                split_chunk(layer, 4, 0)
                norm_heads(layer, 1)
                gate_o(layer, 0)
                for s in GAPS["G", 0]:
                    read_small(layer, s)
                stats(layer, 2)
                finish_gate(layer, 0)
                norm_heads(layer, 2)
                gate_o(layer, 1)
                for s in GAPS["G", 1]:
                    read_small(layer, s)
                stats(layer, 3)
                finish_gate(layer, 1)
                norm_heads(layer, 3)
                stats(layer, 0)
                gate_o(layer, 2)
                norm_heads(layer, 0)
                for s in GAPS["G", 2]:
                    read_small(layer, s)
                stats(layer, 4)
                finish_gate(layer, 2)
                norm_heads(layer, 4)
                gate_o(layer, 3)
                finish_gate(layer, 3)
                for t in range(2):
                    read_turn_lo(layer, ("o", t))
                gate_o(layer, 4)
                finish_gate(layer, 4)
                for t in range(2, 4):
                    read_turn_lo(layer, ("o", t))

                split_chunk(layer, 5, 1)
                read_turn_lo(layer, ("o", 4))
                nc.vector.memset(u[:, :, 0:2], 0.0)

                for ft in range(FT):
                    for half in range(2):
                        n = GROUP["H", ft, half]
                        wait_group(layer, n)
                        dve.wait_ge(scalar_read.sem, scalar_read.at(
                            layer, MIX_SCALAR.index(GROUP["C", ft, half]) + 1))
                        src = mix_bank[n % 3]
                        if half == 0:
                            uu = u[:, ft, 2:2 + HALF]
                            ins = nc.vector.tensor_tensor(uu, uu, src[:, 0:HALF], ALU.mult)
                        else:
                            rest = SEQ - HALF
                            uu = u[:, ft, 2 + HALF:2 + SEQ]
                            nc.vector.tensor_tensor(uu, uu, src[:, 0:rest], ALU.mult)
                            uu = u_sample(ft, 2)
                            ins = nc.vector.tensor_tensor(uu, uu, sample_cols(src[:, rest:HALF]), ALU.mult)
                        ins.then_inc(vector_read.sem, 1)
                    if ft in (0, 1):
                        split_unit(layer, 6, ft, 0)
                dve.wait_ge(vector_read.sem, vector_read.at(layer, MIX_VECTOR.index(GROUP["H", FT - 1, 1]) + 1))
                nc.vector.tensor_copy(tail[:, :, 0:2], u[:, :, SEQ:SEQ + 2])
                streams = u[:, :, SEQ + 2:UPAD].rearrange("p f (b s) -> p f b s", b=NB)[:, :, :, NS:NS + 2]
                nc.vector.tensor_copy(tail[:, :, 2:].rearrange("p f (b r) -> p f b r", b=NB), streams
                                      ).then_inc(tail_ready.sem, 1)

                def lo_part(ft, half):
                    dve.wait_ge(mix_hi.sem, mix_hi.at(layer, 2 * ft + half + 1))
                    cols = slice(half * HALF, (half + 1) * HALF)
                    nc.vector.tensor_tensor(inner_lo[:, FT + ft, cols], z[:, ft % 2, cols],
                                            f(inner_hi[:, FT + ft, cols]), ALU.subtract).then_inc(mix_lo.sem, 1)

                for ft in range(FT):
                    dve.wait_ge(tap0_ready.sem, tap0_ready.at(layer, ft + 1))
                    zp, zs = z[:, ft % 2, 0:SEQ], sample_cols(z[:, ft % 2, SEQ:TOK])
                    for tap in (1, 2):
                        w = conv_taps[:, ft, tap:tap + 1]
                        nc.vector.scalar_tensor_tensor(out=zp, in0=u[:, ft, tap:tap + SEQ], scalar=w, in1=zp,
                                                       op0=ALU.mult, op1=ALU.add)
                        nc.vector.scalar_tensor_tensor(out=zs, in0=u_sample(ft, tap), scalar=w, in1=zs,
                                                       op0=ALU.mult, op1=ALU.add).then_inc(tap_step.sem, 1)
                        dve.wait_ge(tap_step.sem, tap_step.at(layer, 2 * ft + tap))
                    for half in range(2):
                        n = GROUP["B", ft, half]
                        wait_group(layer, n)
                        zz = z[:, ft % 2, half * HALF:(half + 1) * HALF]
                        nc.vector.tensor_tensor(zz, zz, mix_bank[n % 3][:, 0:HALF], ALU.mult
                                                ).then_inc(vector_read.sem, 1)
                    if ft in (0, 1):
                        split_unit(layer, 7, ft, 1)
                    for half in range(2):
                        lo_part(ft, half)

                def add_into_x(n, src, t, dh):
                    dve.wait_ge(group_done.sem, n)
                    xx = x[:, t, dh * 512:(dh + 1) * 512]
                    nc.vector.tensor_tensor(xx, xx, src[:], ALU.add).then_inc(vector_read.sem, 1)

                for t in range(NT):
                    n = GROUP["O", 0, t]
                    add_into_x(group_done.at(layer, n + 1), mix_bank[n % 3], t, 0)
                    if t in (0, 1):
                        split_unit(layer, 8, t, 0)
                for t in range(NT):
                    n = GROUP["O", 1, t]
                    add_into_x(group_done.at(layer, n + 1), mix_bank[n % 3], t, 1)
                    if t < 4:
                        split_unit(layer, 9, t // 2, 1, t % 2)
                    normalise(layer, NT, t, t, 32)
                    if t >= 1:
                        for c in range(2):
                            read_turn_lo(layer, ("n2", t - 1, c))
                for c in range(2):
                    read_turn_lo(layer, ("n2", NT - 1, c))

                def up_block(b, buf, chunk, par):
                    def lo_part(j):
                        half, ft = divmod(j, FT)
                        cols = slice(half * HALF, (half + 1) * HALF)
                        dve.wait_ge(hidden_hi.sem, hidden_hi.at(layer, b * UPS + (j + 1)))
                        nc.vector.tensor_tensor(inner_lo[:, buf * FT + ft, cols], relu[:, j % 4],
                                                f(inner_hi[:, buf * FT + ft, cols]), ALU.subtract
                                                ).then_inc(hidden_lo.sem, 1)

                    for j in range(UPS):
                        dve.wait_ge(scalar_read.sem, scalar_read.at(
                            layer, b * UPS + (len(MIX_SCALAR) + j + 1)))
                        nc.vector.tensor_tensor(relu[:, j % 4], relu[:, j % 4], relu[:, j % 4], ALU.mult
                                                ).then_inc(squared.sem, 1)
                        if j >= 1:
                            lo_part(j - 1)
                        if j in (0, 1):
                            split_unit(layer, chunk, j, par)
                    lo_part(UPS - 1)

                def down_block(d, split=None):
                    last = isinstance(d, int) and d == NBLK - 1
                    start = (PER_LAYER - MIX - DOWNS) if last else 2 * UPS
                    for j in range(DOWNS):
                        dh, p = divmod(j, NT)
                        add_into_x(group_done.at(layer, down_group(d, j + 1)), mlp_bank[(start + j) % 6],
                                   ORDER[p], dh)
                        if last and j == NT - 1:
                            with dve.If(layer < DEPTH - 1):
                                split_first(layer + 1, 0)
                        if last and dh == 1 and 1 <= p < 3:
                            normalise(layer + 1, 0, p - 1, ORDER[p - 1], 16)
                        if last and dh == 1 and p == 3:
                            with dve.If(layer < DEPTH - 1):
                                for c in range(2):
                                    read_turn_lo(layer + 1, ("n1", 0, c))
                            with dve.If(layer > DEPTH - 2):
                                normalise_last(2)
                        if split is not None and j in (0, 1):
                            split_unit(layer, split, j, 0)

                up_block(0, 0, 10, 0)
                with dve.Fori(0, NBLK // 2 - 1) as i:
                    for b in range(2):
                        up_block(i * 2 + (b + 1), (b + 1) % 2, down_chunk(i * 2 + b), 1)
                        down_block(i * 2 + b, up_chunk(i * 2 + (b + 2)))
                up_block(NBLK - 1, 1, down_chunk(NBLK - 2), 1)
                down_block(NBLK - 2, down_chunk(NBLK - 1))
                down_block(NBLK - 1)

            normalise_last(3)
            normalise_last(4, pieces=2)


def shape_constants():
    pos = np.concatenate([np.arange(SEQ), np.tile(256 + np.arange(NS), NB)]).astype(np.float32)
    half = HD // 2
    inv = (10000.0 ** (-np.arange(half, dtype=np.float64) / half)).astype(np.float32)
    ang = (pos[:, None] * inv[None, :]).astype(np.float64)
    cos_sin = np.stack([np.cos(ang), np.sin(ang)], 1).reshape(NT, P, HD).transpose(1, 0, 2)
    g = 1.0 - 2.0 ** (-5.0 - np.arange(H))
    m = np.arange(P)
    scale = HD ** -0.5
    masks, q_decay, k_decay = [], [], []
    for chunk in (P, NS):
        i = m % chunk
        same = (m[:, None] // chunk == m[None, :] // chunk) & (m[:, None] <= m[None, :])
        masks.append((scale * g[None, :, None] ** -(i[:, None, None] + 1.0) * same[:, None, :]).reshape(P, H * P))
        q_decay.append(g[None, :] ** (i[:, None] + 1.0))
        k_decay.append(scale * g[None, :] ** (chunk - 1.0 - i[:, None]))
    stream = (m[:, None] // NS == np.arange(NB)[None, :])
    return np.concatenate([np.eye(P), cos_sin.reshape(P, NT * HD), *masks, *q_decay, *k_decay, stream],
                          1).astype(np.float32)


def kernel(**inputs):
    import concourse.bacc as bacc
    from concourse.bass_utils import run_bass_kernel_spmd

    a = {k: np.ascontiguousarray(v) for k, v in inputs.items()}
    a["norm_rows"] = np.concatenate([a.pop("ln1_w"), a.pop("ln_f_w")[None, :]], 0)
    a["consts"] = shape_constants()
    nc = bacc.Bacc("TRN2", target_bir_lowering=False, num_devices=1, dynamic_dma_scratch_size=1024)
    names = ["x_prompt", "x_sample", "state_ret", "state_conv", "norm_rows", "ln2_w", "w_in", "conv_w",
             "ret_norm_w", "w_out", "w_mlp_up", "w_mlp_down", "consts"]
    args = [nc.dram_tensor("in_" + n, a[n].shape, mybir.dt.float32, kind="ExternalInput").ap() for n in names]
    outs = [("y_p", (1, SEQ, D)), ("y_s", (NB, NS, D)), ("ret_p", (DEPTH, 1, H, HD, HD)), ("conv_p", (DEPTH, 1, 2, CW)),
            ("ret_s", (DEPTH, NB, H, HD, HD)), ("conv_s", (DEPTH, NB, 2, CW))]
    args += [nc.dram_tensor("out_" + n, s, mybir.dt.float32, kind="ExternalOutput").ap() for n, s in outs]
    program(nc, *args)
    r = run_bass_kernel_spmd(nc, [{"in_" + n: a[n] for n in names}], core_ids=[0])
    return tuple(r.results[0]["out_" + n] for n, _ in outs)
```
